# Optimizing a Trainium2 kernel written in Bass

```python
import math
import jax, jax.numpy as jnp
from jax import lax
import numpy as np

D_MODEL = 1024
BATCH = 1
SEQ = 1024
DEPTH = 1

SSD_HEADS = 8
SSD_HEAD_DIM = 64
SSD_INNER = SSD_HEADS * SSD_HEAD_DIM
SSD_GROUPS = 2
SSD_STATE = 128
SSD_CONV = 4
SSD_CHUNK = 128
SSD_XBC = SSD_INNER + 2 * SSD_GROUPS * SSD_STATE
DT_MIN = 0.001
DT_MAX = 0.1
MLA_HEADS = 8
MLA_NOPE = 64
MLA_ROPE = 32
MLA_QK = MLA_NOPE + MLA_ROPE
MLA_V = 64
MLA_Q_RANK = 256
MLA_KV_RANK = 128
MLA_INNER = MLA_HEADS * MLA_V
ROPE_THETA = 10000.0
ATTN_BLOCK = 128
MAX_POS_OFFSET = 4096
D_MIX = SSD_INNER + MLA_INNER
IN_SPLITS = (SSD_INNER, SSD_XBC, SSD_HEADS, MLA_Q_RANK, MLA_KV_RANK, MLA_ROPE)
D_IN_PROJ = sum(IN_SPLITS)
MOE_GROUPS = 4
MOE_EXPERTS_PER_GROUP = 8
MOE_EXPERTS = MOE_GROUPS * MOE_EXPERTS_PER_GROUP
MOE_TOP_K = 2
MOE_FF = 256
N_MOD = 6
EPS = 1e-6

kernel_name = "hymba_ssd_mla_hmoe_block"

def rms_norm(x, g):
    xf = x.astype(jnp.float32)
    y = xf * lax.rsqrt(jnp.mean(xf * xf, axis=-1, keepdims=True) + EPS)
    return (y * g.astype(jnp.float32)).astype(x.dtype)

def causal_depthwise_conv(u, w, b):
    k_w, ch = w.shape
    y = lax.conv_general_dilated(u, w[:, None, :].astype(u.dtype), window_strides=(1,),
                                 padding=[(k_w - 1, 0)],
                                 dimension_numbers=('NWC', 'WIO', 'NWC'),
                                 feature_group_count=ch)
    return y + b

def segsum(a):
    n = a.shape[-1]
    cs = jnp.cumsum(a, axis=-1)
    diff = cs[..., :, None] - cs[..., None, :]
    mask = jnp.tril(jnp.ones((n, n), dtype=bool))
    return jnp.where(mask, diff, -jnp.inf)

def ssd_chunked(x, dt, a, bm, cm):
    b, s, h, p = x.shape
    g, n = bm.shape[-2:]
    r = h // g
    nc = s // SSD_CHUNK
    f32 = jnp.float32
    xd = (x.astype(f32) * dt[..., None]).reshape(b, nc, SSD_CHUNK, g, r, p)
    adt = jnp.moveaxis((dt * a).reshape(b, nc, SSD_CHUNK, g, r), 2, -1)
    bc = bm.astype(f32).reshape(b, nc, SSD_CHUNK, g, n)
    cc = cm.astype(f32).reshape(b, nc, SSD_CHUNK, g, n)
    a_cs = jnp.cumsum(adt, axis=-1)
    decay = jnp.exp(segsum(adt))
    cb = jnp.einsum('bclgn,bcsgn->bcgls', cc, bc)
    y_diag = jnp.einsum('bcgrls,bcsgrp->bclgrp', cb[:, :, :, None] * decay, xd)
    decay_states = jnp.exp(a_cs[..., -1:] - a_cs)
    states = jnp.einsum('bclgn,bcgrl,bclgrp->bcgrpn', bc, decay_states, xd)
    chunk_decay = jnp.exp(a_cs[..., -1])

    def step(carry, inp):
        st, dec = inp
        return carry * dec[..., None, None] + st, carry

    init = jnp.zeros((b, g, r, p, n), f32)
    _, prev = lax.scan(step, init, (jnp.moveaxis(states, 1, 0), jnp.moveaxis(chunk_decay, 1, 0)))
    prev = jnp.moveaxis(prev, 0, 1)
    y_off = jnp.einsum('bclgn,bcgrpn,bcgrl->bclgrp', cc, prev, jnp.exp(a_cs))
    return (y_diag + y_off).reshape(b, s, h, p)

def rope_tables(positions):
    inv = 1.0 / (ROPE_THETA ** (jnp.arange(0, MLA_ROPE, 2, dtype=jnp.float32) / MLA_ROPE))
    ang = positions.astype(jnp.float32)[..., None] * inv
    return jnp.cos(ang), jnp.sin(ang)

def apply_rope(x, cos, sin):
    xf = x.astype(jnp.float32)
    x1, x2 = jnp.split(xf, 2, axis=-1)
    return jnp.concatenate([x1 * cos - x2 * sin, x2 * cos + x1 * sin], axis=-1).astype(x.dtype)

def causal_attention_blocked(q, k, v):
    b, s, h, d = q.shape
    nb = s // ATTN_BLOCK
    scale = d ** -0.5
    qb = jnp.moveaxis(q.reshape(b, nb, ATTN_BLOCK, h, d), 1, 0)
    k_idx = jnp.arange(s)

    def one_block(args):
        q_blk, i = args
        sc = jnp.einsum('bqhd,bkhd->bhqk', q_blk, k).astype(jnp.float32) * scale
        q_idx = i * ATTN_BLOCK + jnp.arange(ATTN_BLOCK)
        sc = jnp.where(k_idx[None, :] <= q_idx[:, None], sc, -jnp.inf)
        pr = jax.nn.softmax(sc, axis=-1).astype(v.dtype)
        return jnp.einsum('bhqk,bkhd->bqhd', pr, v)

    out = lax.map(one_block, (qb, jnp.arange(nb)))
    return jnp.moveaxis(out, 0, 1).reshape(b, s, h, v.shape[-1])

def hybrid_mixer(h, cos, sin, w_in, conv_w, conv_b, dt_bias, a_log, d_skip, ssd_norm,
                 q_norm, w_uq, kv_norm, w_ukv, mla_out_norm, w_out):
    b, s, _ = h.shape
    u = h @ w_in
    cuts = list(np.cumsum(IN_SPLITS)[:-1])
    z, xbc, dt_raw, cq, ckv, k_rope = jnp.split(u, cuts, axis=-1)
    xbc = jax.nn.silu(causal_depthwise_conv(xbc, conv_w, conv_b))
    xs, bs, cs = jnp.split(xbc, [SSD_INNER, SSD_INNER + SSD_GROUPS * SSD_STATE], axis=-1)
    xs = xs.reshape(b, s, SSD_HEADS, SSD_HEAD_DIM)
    bs = bs.reshape(b, s, SSD_GROUPS, SSD_STATE)
    cs = cs.reshape(b, s, SSD_GROUPS, SSD_STATE)
    dt = jax.nn.softplus(dt_raw.astype(jnp.float32) + dt_bias.astype(jnp.float32))
    a = -jnp.exp(a_log.astype(jnp.float32))
    y_ssd = ssd_chunked(xs, dt, a, bs, cs) + d_skip.astype(jnp.float32)[:, None] * xs.astype(jnp.float32)
    y_ssd = y_ssd.reshape(b, s, SSD_INNER).astype(h.dtype)
    y_ssd = rms_norm(y_ssd * jax.nn.silu(z), ssd_norm)
    q = jnp.einsum('bsr,rhd->bshd', rms_norm(cq, q_norm), w_uq)
    q_nope, q_pe = jnp.split(q, [MLA_NOPE], axis=-1)
    kv = jnp.einsum('bsr,rhd->bshd', rms_norm(ckv, kv_norm), w_ukv)
    k_nope, v = jnp.split(kv, [MLA_NOPE], axis=-1)
    q_pe = apply_rope(q_pe, cos[:, :, None, :], sin[:, :, None, :])
    k_pe = apply_rope(k_rope, cos, sin)
    q_full = jnp.concatenate([q_nope, q_pe], axis=-1)
    k_full = jnp.concatenate(
        [k_nope, jnp.broadcast_to(k_pe[:, :, None, :], (b, s, MLA_HEADS, MLA_ROPE))], axis=-1)
    y_mla = causal_attention_blocked(q_full, k_full, v).reshape(b, s, MLA_INNER)
    y_mla = rms_norm(y_mla, mla_out_norm)
    return jnp.concatenate([y_ssd, y_mla], axis=-1) @ w_out

def hierarchical_moe(h, w_group_router, b_group_router, w_expert_router, b_expert_router,
                     w_gate, w_up, w_down):
    b, s, d = h.shape
    t = h.reshape(b * s, d)
    n_tok = t.shape[0]
    g_prob = jax.nn.softmax((t @ w_group_router).astype(jnp.float32)
                            + b_group_router.astype(jnp.float32), axis=-1)
    g_w, g_idx = lax.top_k(g_prob, 1)
    e_logits = (t @ w_expert_router).astype(jnp.float32).reshape(
        n_tok, MOE_GROUPS, MOE_EXPERTS_PER_GROUP) + b_expert_router.astype(jnp.float32)
    e_sel = jnp.take_along_axis(e_logits, g_idx[:, :, None], axis=1)[:, 0]
    e_prob = jax.nn.softmax(e_sel, axis=-1)
    e_w, e_idx = lax.top_k(e_prob, MOE_TOP_K)
    e_w = e_w / jnp.sum(e_w, axis=-1, keepdims=True)
    w = g_w * e_w
    flat_idx = g_idx * MOE_EXPERTS_PER_GROUP + e_idx
    combine = jnp.einsum('tk,tke->te', w, jax.nn.one_hot(flat_idx, MOE_EXPERTS, dtype=jnp.float32))
    gate = jnp.einsum('td,edf->tef', t, w_gate)
    up = jnp.einsum('td,edf->tef', t, w_up)
    hid = (jax.nn.silu(gate) * up * combine[:, :, None].astype(t.dtype))
    out = jnp.einsum('tef,efd->td', hid, w_down)
    return out.reshape(b, s, d).astype(h.dtype)

def setup_inputs(seed: int = 0) -> dict:
    key = jax.random.key(seed)
    ks = jax.random.split(key, 32)
    f32 = jnp.float32
    L = DEPTH

    def nrm(k, shape, scale):
        return jax.random.normal(k, shape, f32) * scale

    def gain(k, n):
        return 1.0 + 0.02 * jax.random.normal(k, (L, n), f32)

    x = nrm(ks[0], (BATCH, SEQ, D_MODEL), 1.0)
    c = nrm(ks[1], (BATCH, D_MODEL), 1.0)
    offset = jax.random.randint(ks[2], (BATCH, 1), 0, MAX_POS_OFFSET, dtype=jnp.int32)
    positions = offset + jnp.arange(SEQ, dtype=jnp.int32)[None, :]
    dt_init = jnp.exp(jax.random.uniform(ks[11], (L, SSD_HEADS), f32,
                                         math.log(DT_MIN), math.log(DT_MAX)))
    return {
        "x": x,
        "c": c,
        "positions": positions,
        "ada_w": nrm(ks[3], (L, D_MODEL, N_MOD * D_MODEL), 0.5 * D_MODEL ** -0.5),
        "ada_b": nrm(ks[4], (L, N_MOD * D_MODEL), 0.02),
        "pre_norm_mix": gain(ks[5], D_MODEL),
        "post_norm_mix": gain(ks[6], D_MODEL),
        "pre_norm_ffn": gain(ks[7], D_MODEL),
        "post_norm_ffn": gain(ks[8], D_MODEL),
        "w_in": nrm(ks[9], (L, D_MODEL, D_IN_PROJ), D_MODEL ** -0.5),
        "conv_w": nrm(ks[10], (L, SSD_CONV, SSD_XBC), SSD_CONV ** -0.5),
        "conv_b": nrm(ks[12], (L, SSD_XBC), 0.01),
        "dt_bias": dt_init + jnp.log(-jnp.expm1(-dt_init)),
        "a_log": jnp.log(jax.random.uniform(ks[13], (L, SSD_HEADS), f32, 1.0, 16.0)),
        "d_skip": 1.0 + 0.1 * jax.random.normal(ks[14], (L, SSD_HEADS), f32),
        "ssd_norm": gain(ks[15], SSD_INNER),
        "q_norm": gain(ks[16], MLA_Q_RANK),
        "w_uq": nrm(ks[17], (L, MLA_Q_RANK, MLA_HEADS, MLA_QK), MLA_Q_RANK ** -0.5),
        "kv_norm": gain(ks[18], MLA_KV_RANK),
        "w_ukv": nrm(ks[19], (L, MLA_KV_RANK, MLA_HEADS, MLA_NOPE + MLA_V), MLA_KV_RANK ** -0.5),
        "mla_out_norm": gain(ks[20], MLA_INNER),
        "w_out": nrm(ks[21], (L, D_MIX, D_MODEL), D_MIX ** -0.5),
        "w_group_router": nrm(ks[22], (L, D_MODEL, MOE_GROUPS), D_MODEL ** -0.5),
        "b_group_router": nrm(ks[23], (L, MOE_GROUPS), 0.01),
        "w_expert_router": nrm(ks[24], (L, D_MODEL, MOE_EXPERTS), D_MODEL ** -0.5),
        "b_expert_router": nrm(ks[25], (L, MOE_GROUPS, MOE_EXPERTS_PER_GROUP), 0.01),
        "w_gate": nrm(ks[26], (L, MOE_EXPERTS, D_MODEL, MOE_FF), D_MODEL ** -0.5),
        "w_up": nrm(ks[27], (L, MOE_EXPERTS, D_MODEL, MOE_FF), D_MODEL ** -0.5),
        "w_down": nrm(ks[28], (L, MOE_EXPERTS, MOE_FF, D_MODEL), MOE_FF ** -0.5),
    }

def reference(x, c, positions, ada_w, ada_b, pre_norm_mix, post_norm_mix, pre_norm_ffn,
              post_norm_ffn, w_in, conv_w, conv_b, dt_bias, a_log, d_skip, ssd_norm,
              q_norm, w_uq, kv_norm, w_ukv, mla_out_norm, w_out, w_group_router,
              b_group_router, w_expert_router, b_expert_router, w_gate, w_up, w_down):
    cos, sin = rope_tables(positions)
    c_act = jax.nn.silu(c)
    for l in range(DEPTH):
        mod = (c_act @ ada_w[l] + ada_b[l])[:, None, :]
        sh1, sc1, g1, sh2, sc2, g2 = jnp.split(mod, N_MOD, axis=-1)
        h = rms_norm(x, pre_norm_mix[l]) * (1.0 + sc1) + sh1
        y = hybrid_mixer(h, cos, sin, w_in[l], conv_w[l], conv_b[l], dt_bias[l], a_log[l],
                         d_skip[l], ssd_norm[l], q_norm[l], w_uq[l], kv_norm[l], w_ukv[l],
                         mla_out_norm[l], w_out[l])
        x = x + g1 * rms_norm(y, post_norm_mix[l])
        h = rms_norm(x, pre_norm_ffn[l]) * (1.0 + sc2) + sh2
        y = hierarchical_moe(h, w_group_router[l], b_group_router[l], w_expert_router[l],
                             b_expert_router[l], w_gate[l], w_up[l], w_down[l])
        x = x + g2 * rms_norm(y, post_norm_ffn[l])
    return x


_drawn_inputs = setup_inputs


def setup_inputs(seed=0):
    import zlib

    import numpy as np

    out = dict(_drawn_inputs(seed))
    spreads = {}
    factors = {'post_norm_ffn': 8.0,
     'conv_b': 3.802,
     'q_norm': 3.272,
     'kv_norm': 2.702,
     'mla_out_norm': 2.81,
     'b_expert_router': 3.75}
    for name, (base, spread) in spreads.items():
        noise = np.random.default_rng([zlib.crc32(name.encode()), seed]).standard_normal(out[name].shape)
        drawn = base * np.exp(spread * noise) if base else spread * noise
        out[name] = __import__('jax').numpy.asarray(drawn.astype(out[name].dtype))
    for name, factor in factors.items():
        out[name] = (out[name] * factor).astype(out[name].dtype)
    return out
```

```python
import math
from contextlib import ExitStack

import numpy as np
import concourse.bass as bass
from concourse import mybir

F32 = mybir.dt.float32
BF16 = mybir.dt.bfloat16
I32 = mybir.dt.int32
ALU = mybir.AluOpType
ACT = mybir.ActivationFunctionType
AX_X = mybir.AxisListType.X

P = 128
EPS = 1e-6
ROPE_THETA = 10000.0
NEG = -1.0e30


def inv_freq_table(n, width):
    return (np.float32(1.0) / np.power(np.float32(ROPE_THETA), np.arange(0, 2 * n, 2, dtype=np.float32)
                                       / np.float32(width))).astype(np.float32)


def hybrid_block(nc, x, c, positions, ada_w, ada_b, pre_norm_mix, post_norm_mix, pre_norm_ffn,
                 post_norm_ffn, w_in, conv_w, conv_b, dt_bias, a_log, d_skip, ssd_norm, q_norm,
                 w_uq, kv_norm, w_ukv, mla_out_norm, w_out, w_group_router, b_group_router,
                 w_expert_router, b_expert_router, w_gate, w_up, w_down, out):
    _, T, D = x.shape
    NT = T // P
    KC = D // P
    H = dt_bias.shape[1]
    TAPS, CH = conv_w.shape[1:]
    NCT = CH // P
    IN_SSD = ssd_norm.shape[1]
    HD = IN_SSD // H
    NX = IN_SSD // P
    G = (CH - IN_SSD) // (2 * P)
    RQ, MH, QK = w_uq.shape[1:]
    RKV = w_ukv.shape[1]
    INNER = mla_out_norm.shape[1]
    V = INNER // MH
    NOPE = w_ukv.shape[3] - V
    ROPE = QK - NOPE
    HR = ROPE // 2
    QC = RQ // P
    REST = H + RQ + RKV + ROPE
    NG, EPG = b_expert_router.shape[1:]
    E = NG * EPG
    FF = w_gate.shape[3]
    FC = FF // P
    PAD = TAPS - 1
    HALF = 512
    NH2 = T // HALF
    SCALE = QK ** -0.5

    ctx = ExitStack()
    with ctx:
        def sem(name):
            return ctx.enter_context(nc.semaphore(name))

        at = [(nc.sbuf_base + 31) // 32 * 32]

        def keep(name, shape, dt=F32):
            n = int(np.prod(shape[1:])) * (2 if dt == BF16 else 4)
            t = nc.alloc_sbuf_tensor_at(name, shape, dt, offset=at[0])
            at[0] += (n + 31) // 32 * 32
            return t

        ident = keep("ident", [P, P])
        ones = keep("ones", [P, P])
        tri = keep("tri", [P, P])
        tri_lt = keep("tri_lt", [P, P])
        iota_row = keep("iota_row", [P, P])
        ident_b = keep("ident_b", [P, P], BF16)
        causal_b = keep("causal_b", [P, P], BF16)
        G1 = keep("G1", [P, D])
        A2 = keep("A2", [P, D])
        B2 = keep("B2", [P, D])
        G2 = keep("G2", [P, D])
        A1 = keep("A1", [P, KC])
        B1 = keep("B1", [P, KC])
        c_col = keep("c_col", [P, KC])
        c_act = keep("c_act", [P, KC])
        pre1_col = keep("pre1_col", [P, KC])
        cat_gain = keep("cat_gain", [P, KC])
        conv_rows = keep("conv_rows", [(TAPS + 1) * NCT, P])
        conv_col = keep("conv_col", [P, (TAPS + 1) * NCT])
        pos_i = keep("pos_i", [NT, P], I32)
        pos_f = keep("pos_f", [NT, P])
        pos_col = keep("pos_col", [P, NT])
        inv_freq = keep("inv_freq", [P, HR])
        cos_t = keep("cos_t", [P, NT, HR])
        sin_t = keep("sin_t", [P, NT, HR])
        ang = keep("ang", [P, NT, HR])
        turn = keep("turn", [P, NT, HR])
        turn_i = keep("turn_i", [P, NT, HR], I32)
        dt_raw = keep("dt_raw", [P, NT, H])
        dtb = keep("dtb", [P, H])
        a_row = keep("a_row", [P, H])
        dsk = keep("dsk", [P, H])
        qn_col = keep("qn_col", [P, QC])
        kvn_col = keep("kvn_col", [P, 1])
        minus_half = keep("minus_half", [P, NT])
        stat = keep("stat", [P, 8, NT])
        rstd = keep("rstd", [P, 8, NT])
        modc = keep("modc", [P, 2 * KC])
        b1_col = keep("b1_col", [P, 2, KC])
        rb_row = keep("rb_row", [P, NG + E])
        row_max = keep("row_max", [P, 2])
        row_sum = keep("row_sum", [P, 2])
        row_inv = keep("row_inv", [P, 2])
        XT = 16
        assert XT * (P + 1) > 2 * T - P
        NTILE = E + XT
        idx_i = keep("idx_i", [P, NTILE], I32)
        dst_i = keep("dst_i", [P, NTILE], I32)
        slot_i = keep("slot_i", [P, 2, NT], I32)
        wts = keep("wts", [P, 2, NT])
        META = XT + 1
        meta_i = keep("meta_i", [P, META], I32)
        tok_id = keep("tok_id", [P, NT])
        gate_w = keep("gate_w", [P, NT])
        REGION = at[0]

        def place(name, off, shape, dt=F32):
            return nc.alloc_sbuf_tensor_at(name, shape, dt, offset=REGION + off)

        W_IN_B = KC * w_in.shape[2] * 4
        R_A = 0
        R_HT = W_IN_B
        R_X = R_HT + KC * T * 4
        R_Z = R_X + (NCT * (T + PAD) * 4 + 31) // 32 * 32
        R_U = R_Z + NT * IN_SSD * 4
        LAT = REST - H
        R_S = R_U + NT * LAT * 4
        R_END = R_S + 24576

        w_in_sb = place("w_in_sb", R_A, [P, KC, w_in.shape[2]])
        hT = place("hT", R_HT, [P, KC, T])
        xbc = place("xbc", R_X, [P, NCT, T + PAD])
        zs = place("zs", R_Z, [P, NT, IN_SSD])
        u2 = place("u2", R_U, [P, NT, LAT])
        x_in = [place(f"x_in{i}", R_Z + 4096 * i, [P, D]) for i in range(2)]
        xn = [place(f"xn{i}", R_Z + 8192 + 4096 * i, [P, D]) for i in range(2)]
        acc = place("acc", R_S, [P, 2 * D])
        ada_first = [place(f"ada_first{i}", R_X + 8192 * i, [P, 2 * D]) for i in range(4)]
        ada_later = [place(f"ada_later{i}", R_S + 8192 * (i + 1), [P, 2 * D]) for i in range(2)]
        conv_tmp = [place(f"conv_tmp{i}", R_S + 16384 + 4096 * i, [P, T]) for i in range(2)]
        junk = place("junk", R_END, [P, D])

        ada_row = place("ada_row", R_U, [1, 2 * D])
        w_uq_sb = place("w_uq_sb", R_S + 8192, [P, QC, MH * QK])
        w_ukv_sb = place("w_ukv_sb", R_S, [P, MH * (NOPE + V)])
        q_sb = place("q_sb", R_A, [P, NT, MH, QK])
        k_sb = place("k_sb", R_A + 24576, [P, NT, MH, QK])
        v_sb = place("v_sb", R_A + 49152, [P, NT, MH, V])
        y_mla = place("y_mla", R_A + 65536, [P, NT, INNER])
        RKC = QC + 1
        c_n = [place(f"c_n{i}", R_A + 81920 + 1536 * i, [P, RKC * P]) for i in range(2)]
        c_T = [place(f"c_T{i}", R_A + 84992 + 1536 * i, [P, RKC, P]) for i in range(2)]
        rope_t = [place(f"rope_t{i}", R_A + 88064 + 512 * i, [P, MH, HR]) for i in range(4)]
        k_pe = place("k_pe", R_A + 90112, [P, NT, ROPE])
        k_head = [place(f"k_head{i}", R_A + 81920 + 3072 * i, [P, NT, QK]) for i in range(2)]
        q_head = [place(f"q_head{i}", R_A + 88064 + 3072 * i, [P, NT, QK]) for i in range(2)]
        qT = [place(f"qT{i}", R_S + 4096 * i, [QK, T]) for i in range(2)]
        kT = [place(f"kT{i}", R_S + 8192 + 4096 * i, [QK, T]) for i in range(2)]
        probs = [place(f"probs{i}", R_S + 16384 + 4096 * i, [P, T]) for i in range(2)]
        probsT = [place(f"probsT{i}", R_U + 4096 * i, [P, T]) for i in range(2)]

        NH = NT * H
        w_out_sb = place("w_out_sb", R_A, [P, KC, D])
        wide2 = lambda name, off, n=2: [place(f"{name}{i}", off + 2048 * i, [P, IN_SSD]) for i in range(n)]
        xd = wide2("xd", R_A + 32768)
        xds = wide2("xds", R_A + 36864)
        xsk = wide2("xsk", R_A + 40960)
        decay = wide2("decay", R_A + 45056, 4)
        y_part = wide2("y_part", R_A + 53248)
        state = wide2("state", R_A + 57344, 1)[0]
        state_d = wide2("state_d", R_A + 59392, 1)[0]
        b_tok = [place(f"b_tok{i}", R_A + 61440 + 1024 * i, [P, G * P]) for i in range(2)]
        cb = [place(f"cb{i}", R_A + 63488 + 1024 * i, [P, G, P]) for i in range(2)]
        slim = [place(f"slim{i}", R_S + 256 * i, [P, NT, H]) for i in range(14)]
        dt_x, dt_abs, dt_e, dt_s, dt_z, dt_r, dt_m, dt_all, adt, acs, tot, dec_in, dec_out, dec_all = slim

        W_B = 24576
        SLOTS = [R_A + 81920 + 4096 * i for i in range(3)] + [R_A + 57344, R_A + 61440] \
            + [R_U + 4096 * i for i in range(3)] + [R_S + 4096 * i for i in range(4)]
        row = lambda name, i, n: [place(f"{name}{j}", SLOTS[i + j], [P, D]) for j in range(n)]
        cat, x_res, y_sc, h2 = row("cat", 0, 2), row("x_res", 2, 2), row("y_sc", 4, 2), row("h2_", 6, 2)
        cat_T = [place(f"cat_T{j}", SLOTS[8 + j], [P, KC, P]) for j in range(2)]
        h2_T = [place(f"h2_T{j}", SLOTS[10 + j], [P, KC, P]) for j in range(2)]
        x2 = place("x2", R_X, [P, NT, D])
        h2_rows = nc.dram_tensor("h2_rows", [T, D], F32).ap()
        y_rows = nc.dram_tensor("y_rows", [2 * T, D], F32).ap()
        w_r = place("w_r", R_S + 16384, [P, KC, NG + E])
        logits = place("logits", R_A + 94208, [P, NT, NG + E])
        rt = [place(f"rt{i}", R_A + 81920 + 1024 * i, [P, NT, E]) for i in range(8)]
        oh1, oh2, lm, cand, both, rank, over, lm2 = rt
        oh1, oh2, lm, cand, both, rank, over, lm2 = (t[:, :, :] for t in rt)
        before = place("before", R_A + 90112, [P, NT + 1, E])[:, :, :]
        row_oh = place("row_oh", R_A + 57344, [P, 2 * NT, P])[:, :, :]
        col_oh = place("col_oh", R_U, [P, 2 * NT, NTILE])[:, :, :]
        cmp = place("cmp", R_U + 3072, [P, XT, E])[:, :, :]
        cmp_n = place("cmp_n", R_U + 5120, [P, E, NT])[:, :, :]
        RS_ = R_U + 6144
        tiny = lambda name, i, shape, dt=F32: place(name, RS_ + 128 * i, shape, dt)
        g_max, m1, m2, mn = (tiny(f"tiny{i}", i, [P, NT])[:, :] for i in range(4))
        g_eq, g_cand, g_oh, g_ex = (tiny(f"tinyg{i}", 4 + i, [P, NT, NG])[:, :, :] for i in range(4))
        g_sum, e2, den = (tiny(f"tinys{i}", 8 + i, [P, NT])[:, :] for i in range(3))
        cnt, n_over, incl, base_t, lo128, dlt, zero32 = (tiny(f"tinyc{i}", 11 + i, [P, E])[:, :] for i in range(7))
        slot_f = tiny("slot_f", 18, [P, 2, NT])[:, :, :]
        col_i = tiny("col_i", 19, [P, 2, NT], I32)[:, :, :]
        row_i = tiny("row_i", 20, [P, 2, NT], I32)[:, :, :]
        col_f = tiny("col_f", 21, [P, 2, NT])[:, :, :]
        row_f = tiny("row_f", 22, [P, 2, NT])[:, :, :]
        thr = tiny("thr", 23, [P, NT])[:, :]
        meta_f = tiny("meta_f", 24, [P, META])[:, :]
        put_f = place("put_f", RS_ + 128 * 26, [P, 2, NTILE])
        place_id = tiny("place_id", 30, [P, 2, NT])[:, :, :]
        W_OFF = [R_A + 32768, R_S, R_A, R_A + 57344]
        w_gu = [place(f"w_gu{i}", o, [P, 2, KC, FF]) for i, o in enumerate(W_OFF)]
        w_dn = [place(f"w_dn{i}", o + 16384, [P, FC, D]) for i, o in enumerate(W_OFF)]
        x_g = [place(f"x_g{i}", R_Z + 4096 * i, [P, D]) for i in range(2)]
        xg_T = [place(f"xg_T{i}", R_Z + 8192 + 4096 * i, [P, KC, P]) for i in range(2)]
        y_e = [place(f"y_e{i}", R_U + 4096 * i, [P, D]) for i in range(2)]
        hid_s = [place(f"hid_s{i}", R_A + 81920 + 1024 * i, [P, FF]) for i in range(2)]
        hid = [place(f"hid{i}", R_A + 83968 + 1024 * i, [P, FF]) for i in range(2)]
        hid_T = [place(f"hid_T{i}", R_A + 86016 + 1024 * i, [P, FC, P]) for i in range(2)]
        idx_now = [place(f"idx_now{i}", R_A + 88064 + 32 * i, [P, 1], I32) for i in range(2)]
        dst_now = [place(f"dst_now{i}", R_A + 88128 + 32 * i, [P, 1], I32) for i in range(2)]
        NY = 4
        y_g = [place(f"y_g{i}", R_A + 8192 * i, [P, 2, D]) for i in range(NY)]
        y_sum = [place(f"y_sum{i}", R_A + 32768 + 4096 * i, [P, D]) for i in range(NY)]

        PS = ctx.enter_context(nc.psum_tensor("PS", [P, 8, HALF], F32))
        BANK = [PS[:, i, :] for i in range(8)]

        NAMES = """small_loaded masks_made x_loaded0 x_loaded1 win_x_loaded win_rest_loaded ada_loaded0 ada_loaded1
            ada_loaded2 ada_loaded3 ada_row_loaded rows_loaded c_ready ada_step acc_ready mod1_ready mod_rows_ready
            mod_summed sq_done rstd_done xn_done xT_done hT_act hT_dve unit_done unit_act unit_dve z_done z_read
            rest_done rest_read conv_done conv_silu consts_T consts_read angle_done trig_done c_sq_done
            w_up_loaded kpe_step kpe_spread cn_done cT_done cT_read q_done q_read kv_done kv_read rope_step
            head_staged qkT_done qkT_read qk_done max_done exp_done pT_done pT_dve pT_act pv_done inv_done
            o_read dt_pos dt_exp a_exp adt_done cums_done cums_read cums_exp ssd_xT ssd_bT ssd_cb ssd_rows
            ssd_diag ssd_off ssd_state ssd_cbm ssd_arg ssd_xd ssd_xsk ssd_m ssd_y1 ssd_prev ssd_b ssd_exp
            ssd_xds ssd_prevd ssd_y w_out_loaded ssd_ysum y_sq_done cat_done catT_done catT_act catT_dve yo_done
            yo_sq y_out x_res_loaded0 x_res_loaded1 x2_done x2_sq h2_half h2_done h2_stored0 h2_stored1 h2T_done
            h2T_act h2T_dve lg_done lg_read w_r_loaded router_exp rt_both ranks_done slots_done idx_done
            idx_read route_act idx_step wgu_loaded0 wgu_loaded1 wgu_loaded2 wgu_loaded3 wdn_loaded0 wdn_loaded1
            wdn_loaded2 wdn_loaded3 xg_loaded0 xg_loaded1 ya_scaled ysum_done ysum_sq o_scaled o_done o_stored0 o_stored1 o_stored2 o_stored3 yg_loaded0 yg_loaded1 yg_loaded2 yg_loaded3 dst_step v_stored v_down v_ya v_yd
            pool_step dve_step""".split()
        S = {n: sem(n) for n in NAMES}
        LATE = """tx_done tx_act tx_dve gu_done silu_done hid_done th_done th_read dn_done ye_act ye_dve ye_stored0
            ye_stored1 v_gu0 v_gu1 v_dn0 v_dn1 v_xg0 v_xg1 v_idx v_tx v_txa v_txd v_gud v_silu v_hid v_th v_thr gathers_begun""".split()
        EARLY = """x_loaded0 x_loaded1 win_x_loaded win_rest_loaded ada_loaded0 ada_loaded1 ada_loaded2 ada_row_loaded
            c_ready ada_step acc_ready mod1_ready mod_rows_ready mod_summed sq_done xn_done xT_done hT_act
            hT_dve unit_done unit_act unit_dve z_done z_read rest_done rest_read conv_done conv_silu consts_T
            consts_read""".split()
        S.update({new: S[old] for new, old in zip(LATE, EARLY, strict=False)})
        assert len(LATE) <= len(EARLY)

        block_in = nc.Block()
        block = block_in.__enter__()

        ROW0 = 2 * D
        PARTS = ada_w.shape[2] // ROW0
        ada_v = ada_w[0].rearrange("(p k) n -> p k n", k=KC)
        win_v = w_in[0].rearrange("(p k) n -> p k n", k=KC)
        XC0, XC1 = IN_SSD, IN_SSD + CH
        col = lambda v: v[0].rearrange("(p k) -> p k", k=v.shape[1] // P)
        rows = lambda v, n=P: v.partition_broadcast(n)

        def ada_place(n):
            if n < KC:
                return ada_first[n % 4], n % 4, n // 4 + 1
            return ada_later[n % 2], n % 2, KC // 4 + (n - KC) // 2 + 1

        SMALL = 15

        @block.sync
        def _(sp):
            def load_ada(n):
                part, k = n // KC, n % KC
                buf, i, _ = ada_place(n)
                if n >= KC + 2:
                    sp.wait_ge(S["ada_step"], n - 1)
                elif 4 <= n < KC:
                    sp.wait_ge(S["ada_step"], n - 3)
                sp.dma_start(buf[:, :], ada_v[:, k, part * ROW0:(part + 1) * ROW0]).then_inc(S[f"ada_loaded{i}"], 16)

            def load_x(t):
                if t >= 2:
                    sp.wait_ge(S["xn_done"], t - 1)
                    sp.wait_ge(S["sq_done"], t - 1)
                sp.dma_start(x_in[t % 2][:, :], x[0, t * P:(t + 1) * P, :]).then_inc(S[f"x_loaded{t % 2}"], 16)

            load_x(0)
            load_x(1)
            for n in range(KC):
                load_ada(n)
            sp.dma_start(w_in_sb[:, :, XC0:XC1], win_v[:, :, XC0:XC1]).then_inc(S["win_x_loaded"], 16)
            for t in range(2, NT):
                load_x(t)
            sp.dma_start(w_in_sb[:, :, 0:XC0], win_v[:, :, 0:XC0]).then_inc(S["win_rest_loaded"], 16)
            sp.dma_start(w_in_sb[:, :, XC1:], win_v[:, :, XC1:]).then_inc(S["win_rest_loaded"], 16)
            for n in range(KC, PARTS * KC):
                if n % KC == 0:
                    if n // KC == 2:
                        sp.wait_ge(S["acc_ready"], 1)
                    sp.dma_start(ada_row[0:1, :], ada_b[0:1, n // KC * ROW0:(n // KC + 1) * ROW0])\
                        .then_inc(S["ada_row_loaded"], 16)
                load_ada(n)
            sp.wait_ge(S["mod_summed"], 4 * (PARTS - 1) + 1)
            sp.dma_start(w_uq_sb[:, :, :], w_uq[0].rearrange("(p k) h d -> p k (h d)", k=QC)).then_inc(S["w_up_loaded"], 16)
            sp.dma_start(w_ukv_sb[:, :], w_ukv[0].rearrange("p h d -> p (h d)")).then_inc(S["w_up_loaded"], 16)

        pool_steps = [0]

        def inverse_root(pool, q, t0, t1, ready, value):
            pool.wait_ge(ready, value)
            pool_steps[0] += 1
            pool.tensor_scalar(rstd[:, q, t0:t1], stat[:, q, t0:t1], EPS, None, ALU.add).then_inc(S["pool_step"], 1)
            pool.wait_ge(S["pool_step"], pool_steps[0])
            pool.tensor_tensor(rstd[:, q, t0:t1], rstd[:, q, t0:t1], minus_half[:, t0:t1], ALU.pow)\
                .then_inc(S["rstd_done"], 1)

        @block.gpsimd
        def _(pool):
            def link(ins):
                pool_steps[0] += 1
                ins.then_inc(S["pool_step"], 1)
                pool.wait_ge(S["pool_step"], pool_steps[0])

            pool.dma_start(c_col[:, :], col(c)).then_inc(S["small_loaded"], 16)
            pool.dma_start(pre1_col[:, :], col(pre_norm_mix)).then_inc(S["small_loaded"], 16)
            half = P // 2
            pool.dma_start(cat_gain[0:half, :], ssd_norm[0].rearrange("(p k) -> p k", k=KC)).then_inc(S["small_loaded"], 16)
            pool.dma_start(cat_gain[half:P, :], mla_out_norm[0].rearrange("(p k) -> p k", k=KC)).then_inc(S["small_loaded"], 16)
            pool.dma_start(conv_rows[0:TAPS * NCT, :], conv_w[0].rearrange("j (n p) -> (j n) p", p=P)).then_inc(S["small_loaded"], 16)
            pool.dma_start(conv_rows[TAPS * NCT:, :], conv_b[0].rearrange("(n p) -> n p", p=P)).then_inc(S["small_loaded"], 16)
            pool.dma_start(pos_i[:, :], positions[0].rearrange("(n p) -> n p", p=P)).then_inc(S["small_loaded"], 16)
            pool.dma_start(dtb[:, :], rows(dt_bias[0])).then_inc(S["small_loaded"], 16)
            pool.dma_start(a_row[:, :], rows(a_log[0])).then_inc(S["small_loaded"], 16)
            pool.dma_start(dsk[:, :], rows(d_skip[0])).then_inc(S["small_loaded"], 16)
            pool.dma_start(qn_col[:, :], col(q_norm)).then_inc(S["small_loaded"], 16)
            pool.dma_start(kvn_col[:, :], col(kv_norm)).then_inc(S["small_loaded"], 16)
            pool.dma_start(b1_col[:, :, :], ada_b[0, 0:ROW0].rearrange("(s p k) -> p s k", s=2, k=KC)).then_inc(S["small_loaded"], 16)
            pool.dma_start(rb_row[:, 0:NG], rows(b_group_router[0])).then_inc(S["small_loaded"], 16)
            pool.dma_start(rb_row[:, NG:], rows(b_expert_router[0].rearrange("g e -> (g e)"))).then_inc(S["small_loaded"], 16)
            for t_, v_ in ((G1, post_norm_mix), (A2, pre_norm_ffn), (G2, post_norm_ffn)):
                pool.dma_start(t_[:, :], rows(v_[0])).then_inc(S["rows_loaded"], 16)

            pool.memset(ones[:, :], 1.0)
            pool.memset(minus_half[:, :], -0.5)
            for j in range(HR):
                pool.memset(inv_freq[:, j:j + 1], float(inv_freq_table(HR, ROPE)[j]))
            pool.iota(iota_row[:, :], pattern=[[1, P]], base=0, channel_multiplier=0,
                      allow_small_or_imprecise_dtypes=True)
            pool.iota(tok_id[:, :], pattern=[[P, NT]], base=0, channel_multiplier=1,
                      allow_small_or_imprecise_dtypes=True)
            link(pool.memset(causal_b[:, :], 0.0))
            pool.affine_select(out=ident[:, :], in_=ones[:, :], pattern=[[-1, P]], compare_op=ALU.is_equal,
                               fill=0.0, base=0, channel_multiplier=1)
            pool.affine_select(out=tri[:, :], in_=ones[:, :], pattern=[[1, P]], compare_op=ALU.is_ge,
                               fill=0.0, base=0, channel_multiplier=-1)
            pool.affine_select(out=tri_lt[:, :], in_=ones[:, :], pattern=[[1, P]], compare_op=ALU.is_gt,
                               fill=0.0, base=0, channel_multiplier=-1)
            pool.affine_select(out=ident_b[:, :], in_=ones[:, :], pattern=[[-1, P]], compare_op=ALU.is_equal,
                               fill=0.0, base=0, channel_multiplier=1)
            pool.affine_select(out=causal_b[:, :], in_=causal_b[:, :], pattern=[[-1, P]], compare_op=ALU.is_ge,
                               fill=NEG, base=0, channel_multiplier=1).then_inc(S["masks_made"], 1)

            for t in range(NT):
                inverse_root(pool, 0, t, t + 1, S["sq_done"], t + 1)
            for q in (1, 2):
                inverse_root(pool, q, 0, NT, S["c_sq_done"], 2 * NT)

        @block.scalar
        def _(act):
            act.wait_ge(S["small_loaded"], 16 * SMALL)
            act.activation(c_act[:, :], c_col[:, :], ACT.Silu).then_inc(S["c_ready"], 1)

            def mean_square(t):
                act.wait_ge(S[f"x_loaded{t % 2}"], 16 * (t // 2 + 1))
                if t:
                    act.wait_ge(S["sq_done"], t)
                act.activation(junk[:, :], x_in[t % 2][:, :], ACT.Square, scale=D ** -0.5,
                               accum_out=stat[:, 0, t:t + 1]).then_inc(S["sq_done"], 1)

            def hT_half(t):
                act.wait_ge(S["xT_done"], t + 1)
                if t == 0:
                    act.wait_ge(S["mod1_ready"], 1)
                for k in range(KC // 2):
                    last = act.activation(hT[:, k, t * P:(t + 1) * P], BANK[t % 2 * 2][:, k * P:(k + 1) * P],
                                          ACT.Identity, scale=A1[:, k:k + 1], bias=B1[:, k:k + 1])
                last.then_inc(S["hT_act"], 1)

            mean_square(0)
            mean_square(1)
            for t in range(NT):
                hT_half(t)
                if t + 2 < NT:
                    mean_square(t + 2)
            for n in range(0, NH2 * NCT, 2):
                hh, ct = n // NCT, n % NCT
                act.wait_ge(S["unit_done"], n + 1)
                act.activation(xbc[:, ct, PAD + hh * HALF:PAD + (hh + 1) * HALF], BANK[4 + n % 4][:, :],
                               ACT.Copy).then_inc(S["unit_act"], 1)
            for t in range(NT):
                act.wait_ge(S["z_done"], t + 1)
                if t == 0:
                    act.wait_ge(S["xT_done"], NT)
                act.activation(zs[:, t, :], BANK[t % 2][:, 0:IN_SSD], ACT.Silu).then_inc(S["z_read"], 1)
                if t >= 1:
                    act.wait_ge(S["conv_done"], t)
                    act.activation(xbc[:, t - 1, PAD:], conv_tmp[(t - 1) % 2][:, :], ACT.Silu).then_inc(S["conv_silu"], 1)
            for t in range(NT):
                act.wait_ge(S["rest_read"], t + 1)
                if t:
                    act.wait_ge(S["c_sq_done"], 2 * t)
                act.activation(junk[:, 0:RQ], u2[:, t, 0:RQ], ACT.Square, scale=RQ ** -0.5,
                               accum_out=stat[:, 1, t:t + 1]).then_inc(S["c_sq_done"], 1)
                act.activation(junk[:, RQ:RQ + RKV], u2[:, t, RQ:RQ + RKV], ACT.Square, scale=RKV ** -0.5,
                               accum_out=stat[:, 2, t:t + 1]).then_inc(S["c_sq_done"], 1)
            act.wait_ge(S["conv_done"], NT)
            act.activation(xbc[:, NT - 1, PAD:], conv_tmp[(NT - 1) % 2][:, :], ACT.Silu).then_inc(S["conv_silu"], 1)
            act.wait_ge(S["angle_done"], 2)
            act.activation(sin_t[:, :, :], sin_t[:, :, :], ACT.Sin)
            act.activation(cos_t[:, :, :], cos_t[:, :, :], ACT.Sin).then_inc(S["trig_done"], 1)

        step_dve = [0]

        @block.vector
        def _(dve):
            step = step_dve

            def mark(ins):
                step[0] += 1
                ins.then_inc(S["dve_step"], 1)
                return step[0]

            def link(ins):
                dve.wait_ge(S["dve_step"], mark(ins))

            def normed(t):
                dve.wait_ge(S["rstd_done"], t + 1)
                if t >= 2:
                    dve.wait_ge(S["xT_done"], t - 1)
                dve.tensor_scalar(xn[t % 2][:, :], x_in[t % 2][:, :], rstd[:, 0, t:t + 1], None, ALU.mult)\
                    .then_inc(S["xn_done"], 1)

            def ada_chunk(n):
                part, k = n // KC, n % KC
                buf, i, loads = ada_place(n)
                dve.wait_ge(S[f"ada_loaded{i}"], 16 * loads)
                if k == 0:
                    if part:
                        dve.wait_ge(S["mod_summed"], 4 * part - 3)
                    ins = dve.tensor_scalar(acc[:, :], buf[:, :], c_act[:, 0:1], None, ALU.mult)
                else:
                    ins = dve.scalar_tensor_tensor(acc[:, :], buf[:, :], c_act[:, k:k + 1], acc[:, :],
                                                   ALU.mult, ALU.add)
                ins.then_inc(S["ada_step"], 1)
                if k < KC - 1:
                    dve.wait_ge(S["ada_step"], n + 1)
            normed(0)
            normed(1)
            dve.wait_ge(S["c_ready"], 1)
            for n in range(KC):
                ada_chunk(n)
            dve.wait_ge(S["small_loaded"], 16 * SMALL)
            dve.tensor_copy(pos_f[:, :], pos_i[:, :]).then_inc(S["consts_T"], 1)
            dve.wait_ge(S["mod_summed"], 1)
            link(dve.tensor_tensor(modc[:, :], BANK[4][:, 0:2 * KC], b1_col[:, :, :].rearrange("p s k -> p (s k)"), ALU.add))
            dve.tensor_copy(B1[:, :], modc[:, 0:KC])
            dve.scalar_tensor_tensor(A1[:, :], modc[:, KC:2 * KC], 1.0, pre1_col[:, :], ALU.add, ALU.mult)\
                .then_inc(S["mod1_ready"], 1)
            dve.wait_ge(S["mod1_ready"], 1)
            dve.wait_ge(S["consts_T"], 2)
            dve.tensor_copy(conv_col[:, :], BANK[5][:, 0:(TAPS + 1) * NCT])
            dve.tensor_copy(pos_col[:, :], BANK[5][:, P:P + NT]).then_inc(S["consts_read"], 1)

            def hT_half(t):
                dve.wait_ge(S["xT_done"], t + 1)
                for k in range(KC // 2, KC):
                    last = dve.tensor_scalar(hT[:, k, t * P:(t + 1) * P],
                                             BANK[t % 2 * 2 + 1][:, (k - KC // 2) * P:(k - KC // 2 + 1) * P],
                                             A1[:, k:k + 1], B1[:, k:k + 1], ALU.mult, ALU.add)
                last.then_inc(S["hT_dve"], 1)

            for t in range(NT):
                hT_half(t)
                if t + 2 < NT:
                    normed(t + 2)

            def add_bias_row(part):
                dve.wait_ge(S["ada_step"], (part + 1) * KC)
                dve.wait_ge(S["ada_row_loaded"], 16 * part)
                dve.tensor_tensor(acc[0:1, :], acc[0:1, :], ada_row[0:1, :], ALU.add).then_inc(S["acc_ready"], 1)

            def mod_rows(part):
                dve.wait_ge(S["rows_loaded"], 48)
                first, second = ((G1, B2), (A2, G2))[part - 1]
                for q in range(4):
                    b = BANK[2 + q % 2]
                    o = (first if q < 2 else second)[:, q % 2 * HALF:(q % 2 + 1) * HALF]
                    dve.wait_ge(S["mod_summed"], 4 * part - 3 + q + 1)
                    if part == 1 and q >= 2:
                        ins = dve.tensor_copy(o, b)
                    elif part == 2 and q < 2:
                        ins = dve.scalar_tensor_tensor(o, b, 1.0, o, ALU.add, ALU.mult)
                    else:
                        ins = dve.tensor_tensor(o, b, o, ALU.mult)
                    ins.then_inc(S["mod_rows_ready"], 1)

            dve.memset(xbc[:, :, 0:PAD], 0.0)
            done = KC
            for n in range(NH2 * NCT):
                hh, ct = n // NCT, n % NCT
                if n % 2:
                    dve.wait_ge(S["unit_done"], n + 1)
                    dve.tensor_copy(xbc[:, ct, PAD + hh * HALF:PAD + (hh + 1) * HALF], BANK[4 + n % 4][:, :])\
                        .then_inc(S["unit_dve"], 1)
                    for _ in range(2):
                        ada_chunk(done)
                        done += 1
                        if done % KC == 0:
                            add_bias_row(done // KC - 1)
                if n == NCT:
                    mod_rows(1)
            dve.wait_ge(S["small_loaded"], 16 * SMALL)

            dve.wait_ge(S["acc_ready"], PARTS - 1)
            for t in range(NT):
                dve.wait_ge(S["rest_done"], t + 1)
                dve.tensor_copy(dt_raw[:, t, :], BANK[6 + t % 2][:, 0:H])
                dve.tensor_copy(u2[:, t, :], BANK[6 + t % 2][:, H:REST]).then_inc(S["rest_read"], 1)
                if t == 0:
                    mod_rows(2)
                ct = t
                if ct >= 2:
                    dve.wait_ge(S["conv_silu"], ct - 1)
                if ct == 0:
                    dve.wait_ge(S["unit_act"], NH2 * NCT // 2)
                w = lambda j: conv_col[:, j * NCT + ct:j * NCT + ct + 1]
                o = conv_tmp[ct % 2][:, :]
                link(dve.tensor_scalar(o, xbc[:, ct, PAD:], w(PAD), conv_col[:, TAPS * NCT + ct:TAPS * NCT + ct + 1],
                                       ALU.mult, ALU.add))
                for j in range(PAD):
                    ins = dve.scalar_tensor_tensor(o, xbc[:, ct, j:j + T], w(j), o, ALU.mult, ALU.add)
                    if j < PAD - 1:
                        link(ins)
                ins.then_inc(S["conv_done"], 1)

            turn1, turn2 = 6.28125, float(np.float32(int((2 * math.pi - 6.28125) * 2 ** 20) / 2 ** 20))
            turn3 = 2 * math.pi - turn1 - turn2
            wide = [P, NT, HR]
            link(dve.tensor_tensor(ang[:, :, :], inv_freq[:, :].unsqueeze(1).to_broadcast(wide),
                                   pos_col[:, :].unsqueeze(2).to_broadcast(wide), ALU.mult))
            for o, quarter in ((sin_t, 0.0), (cos_t, 0.25)):
                link(dve.tensor_scalar(turn[:, :, :], ang[:, :, :], 0.5 / math.pi, quarter, ALU.mult, ALU.add))
                link(dve.tensor_copy(turn_i[:, :, :], turn[:, :, :]))
                link(dve.tensor_copy(turn[:, :, :], turn_i[:, :, :]))
                link(dve.scalar_tensor_tensor(o[:, :, :], turn[:, :, :], -turn1, ang[:, :, :], ALU.mult, ALU.add))
                for part in (turn2, turn3):
                    link(dve.scalar_tensor_tensor(o[:, :, :], turn[:, :, :], -part, o[:, :, :], ALU.mult, ALU.add))
                link(dve.tensor_scalar(o[:, :, :], o[:, :, :], quarter * 2 * math.pi, 3.1415925, ALU.add, ALU.min))
                dve.tensor_scalar(o[:, :, :], o[:, :, :], -3.1415925, None, ALU.max).then_inc(S["angle_done"], 1)
            
        @block.tensor
        def _(pe):
            pe.wait_ge(S["masks_made"], 1)
            for t in range(NT):
                pe.wait_ge(S["xn_done"], t + 1)
                if t >= 2:
                    pe.wait_ge(S["hT_act"], t - 1)
                    pe.wait_ge(S["hT_dve"], t - 1)
                for k in range(KC):
                    last = pe.transpose(BANK[t % 2 * 2 + k // 4][:, k % 4 * P:(k % 4 + 1) * P], xn[t % 2][:, k::KC], ident[:, :])
                last.then_inc(S["xT_done"], 1)
                if t == 1:
                    pe.wait_ge(S["ada_step"], KC)
                    for q in range(2 * KC):
                        a0 = q // KC * D + q % KC
                        last = pe.matmul(BANK[4][:, q:q + 1], acc[:, a0:a0 + D - KC + 1:KC], ones[:, 0:1],
                                         start=True, stop=True)
                    last.then_inc(S["mod_summed"], 1)
                    pe.wait_ge(S["consts_T"], 1)
                    n = (TAPS + 1) * NCT
                    pe.transpose(BANK[5][:, 0:n], conv_rows[:, :], ident[0:n, 0:n])
                    pe.transpose(BANK[5][:, P:P + NT], pos_f[:, :], ident[0:NT, 0:NT]).then_inc(S["consts_T"], 1)

            def mod_sum(part):
                pe.wait_ge(S["acc_ready"], part)
                if part == 1:
                    pe.wait_ge(S["hT_act"], NT)
                    pe.wait_ge(S["hT_dve"], NT)
                for q in range(4):
                    b = 2 + q % 2
                    if (part - 1) * 4 + q >= 2:
                        pe.wait_ge(S["mod_rows_ready"], (part - 1) * 4 + q - 1)
                    last = pe.matmul(BANK[b][:, :], ones[:, :], acc[:, q * HALF:(q + 1) * HALF], start=True, stop=True)
                    last.then_inc(S["mod_summed"], 1)

            pe.wait_ge(S["win_x_loaded"], 16)
            pe.wait_ge(S["consts_read"], 1)
            for n in range(NH2 * NCT):
                hh, ct = n // NCT, n % NCT
                if ct == 0:
                    pe.wait_ge(S["hT_act"], (hh + 1) * HALF // P)
                    pe.wait_ge(S["hT_dve"], (hh + 1) * HALF // P)
                if n >= 4:
                    pe.wait_ge(S["unit_dve"] if n % 2 else S["unit_act"], n // 2 - 1)
                for k in range(KC):
                    last = pe.matmul(BANK[4 + n % 4][:, :], w_in_sb[:, k, XC0 + ct * P:XC0 + (ct + 1) * P],
                                     hT[:, k, hh * HALF:(hh + 1) * HALF], start=(k == 0), stop=(k == KC - 1))
                last.then_inc(S["unit_done"], 1)
                if n == NCT:
                    mod_sum(1)
            pe.wait_ge(S["win_rest_loaded"], 32)
            for t in range(NT):
                if t >= 2:
                    pe.wait_ge(S["z_read"], t - 1)
                for k in range(KC):
                    last = pe.matmul(BANK[t % 2][:, 0:IN_SSD], hT[:, k, t * P:(t + 1) * P], w_in_sb[:, k, 0:IN_SSD],
                                     start=(k == 0), stop=(k == KC - 1))
                last.then_inc(S["z_done"], 1)
                if t >= 2:
                    pe.wait_ge(S["rest_read"], t - 1)
                elif t == 0:
                    pe.wait_ge(S["unit_act"], NCT)
                    pe.wait_ge(S["unit_dve"], NCT)
                for k in range(KC):
                    last = pe.matmul(BANK[6 + t % 2][:, 0:REST], hT[:, k, t * P:(t + 1) * P], w_in_sb[:, k, XC1:],
                                     start=(k == 0), stop=(k == KC - 1))
                last.then_inc(S["rest_done"], 1)
                if t == 0:
                    mod_sum(2)

        block_in.__exit__(None, None, None)


        CREDIT = {"qkT_done": 8, "qkT_read": 1, "qk_done": 2 * NT, "exp_done": 2, "pT_done": 2,
                  "pT_dve": 1, "pT_act": 1, "pv_done": 2, "o_read": 2}

        def seen(eng, name, value):
            eng.wait_ge(S[name], value + CREDIT.get(name, 0))

        QA = HALF // QK
        KA = HALF // (NOPE + V)
        UNITS = 2 * NT

        with nc.Block() as block:
            def steps(eng, pair):
                with eng.Fori(0, MH // 2 - 1) as i:
                    pair(i * 2, False)
                pair(MH - 2, True)

            def tile_of(g):
                return NT - 1 - g % NT

            @block.gpsimd
            def _(pool):
                for n, v in CREDIT.items():
                    pool.sem_inc(S[n], v)
                pool.wait_ge(S["kpe_step"], 6)
                pool.tensor_copy(k_sb[:, :, :, NOPE:], k_pe[:, :, :].unsqueeze(2).to_broadcast([P, NT, MH, ROPE]))\
                    .then_inc(S["kpe_spread"], 1)

                def stage(h, u, first=False):
                    if not first:
                        seen(pool, "qkT_done", (h - 1) * 4)
                    pool.wait_ge(S["kpe_spread"], 1)
                    pool.tensor_copy(q_head[u][:, :, :], q_sb[:, :, bass.ds(h, 1), :].rearrange("p t a d -> p t (a d)"))
                    pool.tensor_copy(k_head[u][:, :, :], k_sb[:, :, bass.ds(h, 1), :].rearrange("p t a d -> p t (a d)"))\
                        .then_inc(S["head_staged"], 1)

                pool.wait_ge(S["rope_step"], 6 * NT)
                pool.wait_ge(S["kv_read"], 4 * NT)
                stage(0, 0, True)
                stage(1, 1, True)
                with pool.Fori(0, MH // 2 - 1) as i:
                    for u in range(2):
                        stage(i * 2 + 2 + u, u)

            @block.scalar
            def _(act):
                def latent_T(t):
                    act.wait_ge(S["cT_done"], t + 1)
                    if t >= 2:
                        act.wait_ge(S["kv_done"], 2 * (t - 1))
                    for k in range(QC):
                        act.activation(c_T[t % 2][:, k, :], BANK[t % 2][:, k * P:(k + 1) * P], ACT.Copy,
                                       scale=qn_col[:, k:k + 1])
                    act.activation(c_T[t % 2][:, QC, :], BANK[t % 2][:, QC * P:RKC * P], ACT.Copy,
                                   scale=kvn_col[:, :]).then_inc(S["cT_read"], 1)

                latent_T(0)
                for t in range(NT):
                    if t + 1 < NT:
                        latent_T(t + 1)
                    for j, (h0, h1) in enumerate(((0, QA), (QA, MH))):
                        act.wait_ge(S["q_done"], 2 * t + j + 1)
                        act.activation(q_sb[:, t, h0:h1, :], BANK[2 + j][:, 0:(h1 - h0) * QK], ACT.Copy, scale=SCALE)\
                            .then_inc(S["q_read"], 1)

                def turned(h, r, u):
                    seen(act, "qkT_done", h * 4 + r + 1)
                    seen(act, "qk_done", (h - 1) * NT)
                    act.activation((qT if r < 2 else kT)[u][:, r % 2 * HALF:(r % 2 + 1) * HALF], BANK[6][0:QK, :], ACT.Copy)\
                        .then_inc(S["qkT_read"], 1)

                def pair(h0, last):
                    for st in range(UNITS + 2):
                        if st < UNITS:
                            g, b = h0 * NT + st, st % 2
                            n = (tile_of(st) + 1) * P
                            act.wait_ge(S["max_done"], g + 1)
                            seen(act, "pT_done", g - 1)
                            act.activation(probs[b][:, 0:n], PS[:, 2 * b:2 * b + 2, :].rearrange("p a n -> p (a n)")[:, 0:n],
                                           ACT.Exp, bias=row_max[:, b:b + 1], accum_out=row_sum[:, b:b + 1])\
                                .then_inc(S["exp_done"], 1)
                            if st % NT in (2, 6) and not (last and st >= NT):
                                turned(h0 + 1 + st // NT, st % NT // 2, (1 + st // NT) % 2)
                        if 1 <= st <= UNITS and tile_of(st - 1) >= 4:
                            g, b = h0 * NT + st - 1, (st - 1) % 2
                            n = (tile_of(st - 1) + 1) * P
                            seen(act, "pT_done", g + 1)
                            seen(act, "pv_done", g - 1)
                            act.activation(probsT[b][:, HALF:n], BANK[5][:, 0:n - HALF], ACT.Copy).then_inc(S["pT_act"], 1)
                        if st >= 2:
                            g, b = h0 * NT + st - 2, st % 2
                            i = tile_of(st - 2)
                            h = h0 + (st - 2) // NT
                            act.wait_ge(S["inv_done"], g + 1)
                            seen(act, "pv_done", g + 1)
                            act.activation(y_mla[:, i, bass.ds(h * V, V)], BANK[7][:, 0:V], ACT.Copy,
                                           scale=row_inv[:, b:b + 1]).then_inc(S["o_read"], 1)

                turned(0, 1, 0)
                turned(0, 3, 0)
                steps(act, pair)

            @block.vector
            def _(dve):
                dve.wait_ge(S["trig_done"], 1)

                def rotate(x1, x2, cs, sn, o1, o2, tmp, step, before):
                    for i, (a, b_) in enumerate(((x1, cs), (x2, sn), (x2, cs), (x1, sn))):
                        dve.tensor_tensor(tmp[i], a, b_, ALU.mult).then_inc(step, 1)
                    dve.wait_ge(step, before + 4)
                    dve.tensor_tensor(o1, tmp[0], tmp[1], ALU.subtract).then_inc(step, 1)
                    dve.tensor_tensor(o2, tmp[2], tmp[3], ALU.add).then_inc(step, 1)

                kr = u2[:, :, RQ + RKV:]
                flat = [rope_t[i][:, :, :] for i in range(4)]
                assert NT == MH
                rotate(kr[:, :, 0:HR], kr[:, :, HR:], cos_t[:, :, :], sin_t[:, :, :],
                       k_pe[:, :, 0:HR], k_pe[:, :, HR:], flat, S["kpe_step"], 0)
                dve.wait_ge(S["kpe_step"], 6)
                dve.wait_ge(S["rstd_done"], NT + 2)

                def normed(t):
                    if t >= 2:
                        dve.wait_ge(S["cT_done"], t - 1)
                    dve.tensor_scalar(c_n[t % 2][:, 0:RQ], u2[:, t, 0:RQ], rstd[:, 1, t:t + 1], None, ALU.mult)
                    dve.tensor_scalar(c_n[t % 2][:, RQ:], u2[:, t, RQ:RQ + RKV], rstd[:, 2, t:t + 1], None,
                                      ALU.mult).then_inc(S["cn_done"], 1)

                normed(0)
                normed(1)
                for t in range(NT):
                    if t + 2 < NT:
                        normed(t + 2)
                    for j in range(2):
                        dve.wait_ge(S["kv_done"], 2 * t + j + 1)
                        kv = BANK[4 + j].rearrange("p (h d) -> p h d", d=NOPE + V)
                        dve.tensor_copy(k_sb[:, t, j * KA:(j + 1) * KA, 0:NOPE], kv[:, :, 0:NOPE]).then_inc(S["kv_read"], 1)
                        dve.tensor_copy(v_sb[:, t, j * KA:(j + 1) * KA, :], kv[:, :, NOPE:]).then_inc(S["kv_read"], 1)
                    dve.wait_ge(S["q_read"], 2 * t + 2)
                    if t:
                        dve.wait_ge(S["rope_step"], 6 * t)
                    rotate(q_sb[:, t, :, NOPE:NOPE + HR], q_sb[:, t, :, NOPE + HR:],
                           cos_t[:, t:t + 1, :].to_broadcast([P, MH, HR]), sin_t[:, t:t + 1, :].to_broadcast([P, MH, HR]),
                           q_sb[:, t, :, NOPE:NOPE + HR], q_sb[:, t, :, NOPE + HR:], flat, S["rope_step"], 6 * t)

                def turned(h, r, u):
                    seen(dve, "qkT_done", h * 4 + r + 1)
                    seen(dve, "qk_done", (h - 1) * NT)
                    dve.tensor_copy((qT if r < 2 else kT)[u][:, r % 2 * HALF:(r % 2 + 1) * HALF], BANK[6][0:QK, :])\
                        .then_inc(S["qkT_read"], 1)

                def pair(h0, last):
                    for st in range(UNITS + 1):
                        if st < UNITS:
                            g, b = h0 * NT + st, st % 2
                            n = (tile_of(st) + 1) * P
                            seen(dve, "qk_done", g + 1)
                            dve.tensor_reduce(row_max[:, b:b + 1], PS[:, 2 * b:2 * b + 2, :].rearrange("p a n -> p (a n)")[:, 0:n],
                                              AX_X, ALU.max, negate=True).then_inc(S["max_done"], 1)
                            if st % NT in (0, 4) and not (last and st >= NT):
                                turned(h0 + 1 + st // NT, st % NT // 2, (1 + st // NT) % 2)
                        if st >= 1:
                            g, b = h0 * NT + st - 1, (st - 1) % 2
                            n = min((tile_of(st - 1) + 1) * P, HALF)
                            seen(dve, "exp_done", g + 1)
                            seen(dve, "o_read", g - 1)
                            dve.reciprocal(row_inv[:, b:b + 1], row_sum[:, b:b + 1]).then_inc(S["inv_done"], 1)
                            seen(dve, "pT_done", g + 1)
                            seen(dve, "pv_done", g - 1)
                            dve.tensor_copy(probsT[b][:, 0:n], BANK[4][:, 0:n]).then_inc(S["pT_dve"], 1)

                turned(0, 0, 0)
                turned(0, 2, 0)
                steps(dve, pair)

            @block.tensor
            def _(pe):
                pe.wait_ge(S["w_up_loaded"], 32)

                def latent_T(t):
                    pe.wait_ge(S["cn_done"], t + 1)
                    if t >= 2:
                        pe.wait_ge(S["cT_read"], t - 1)
                    for k in range(RKC):
                        src = c_n[t % 2][:, k:RQ:QC] if k < QC else c_n[t % 2][:, RQ:]
                        last = pe.transpose(BANK[t % 2][:, k * P:(k + 1) * P], src, ident[:, :])
                    last.then_inc(S["cT_done"], 1)

                latent_T(0)
                for t in range(NT):
                    if t + 1 < NT:
                        latent_T(t + 1)
                    pe.wait_ge(S["cT_read"], t + 1)
                    for j, (h0, h1) in enumerate(((0, QA), (QA, MH))):
                        if t:
                            pe.wait_ge(S["q_read"], 2 * t - 1 + j)
                        for k in range(QC):
                            last = pe.matmul(BANK[2 + j][:, 0:(h1 - h0) * QK], c_T[t % 2][:, k, :],
                                             w_uq_sb[:, k, h0 * QK:h1 * QK], start=(k == 0), stop=(k == QC - 1))
                        last.then_inc(S["q_done"], 1)
                    for j in range(2):
                        if t:
                            pe.wait_ge(S["kv_read"], 4 * t - 2 + 2 * j)
                        pe.matmul(BANK[4 + j], c_T[t % 2][:, QC, :], w_ukv_sb[:, j * HALF:(j + 1) * HALF],
                                  start=True, stop=True).then_inc(S["kv_done"], 1)

                pe.wait_ge(S["kv_read"], 4 * NT)
                pe.wait_ge(S["q_read"], 2 * NT)

                def turn_head(h, r, u):
                    pe.wait_ge(S["head_staged"], h + 1)
                    seen(pe, "qkT_read", h * 4 + r)
                    src = (q_head if r < 2 else k_head)[u]
                    for j in range(4):
                        last = pe.transpose(BANK[6][0:QK, j * P:(j + 1) * P], src[:, r % 2 * 4 + j, :], ident[:, :])
                    last.then_inc(S["qkT_done"], 1)

                def pair(h0, last_pair):
                    for st in range(UNITS + 2):
                        if st < UNITS:
                            g, b, u, i = h0 * NT + st, st % 2, st // NT, tile_of(st)
                            if st % NT == 0:
                                seen(pe, "qkT_read", (h0 + u) * 4 + 4)
                            seen(pe, "exp_done", g - 1)
                            for c0 in range(0, (i + 1) * P, HALF):
                                c1 = min(c0 + HALF, (i + 1) * P)
                                pe.matmul(BANK[2 * b + c0 // HALF][:, 0:c1 - c0], qT[u][:, i * P:(i + 1) * P],
                                          kT[u][:, c0:c1], start=True, stop=c1 < (i + 1) * P)
                            pe.matmul(BANK[2 * b + i // 4][:, i % 4 * P:(i % 4 + 1) * P], ident_b[:, :], causal_b[:, :],
                                      start=False, stop=True).then_inc(S["qk_done"], 1)
                            if st % NT in (0, 2, 4, 6) and not (last_pair and st >= NT):
                                turn_head(h0 + 1 + st // NT, st % NT // 2, (1 + st // NT) % 2)
                        if 1 <= st <= UNITS:
                            g, b, i = h0 * NT + st - 1, (st - 1) % 2, tile_of(st - 1)
                            seen(pe, "exp_done", g + 1)
                            seen(pe, "pT_dve", g)
                            if i >= 4:
                                seen(pe, "pT_act", (h0 + (st - 1) // NT) * 4 + (st - 1) % NT)
                            for j in range(i + 1):
                                last = pe.transpose(BANK[4 + j // 4][:, j % 4 * P:(j % 4 + 1) * P],
                                                    probs[b][:, j * P:(j + 1) * P], ident[:, :])
                            last.then_inc(S["pT_done"], 1)
                        if st >= 2:
                            g, b, i = h0 * NT + st - 2, st % 2, tile_of(st - 2)
                            h = h0 + (st - 2) // NT
                            seen(pe, "pT_dve", g + 1)
                            if i >= 4:
                                seen(pe, "pT_act", h * 4 + (st - 2) % NT + 1)
                            seen(pe, "o_read", g)
                            for j in range(i + 1):
                                last = pe.matmul(BANK[7][:, 0:V], probsT[b][:, j * P:(j + 1) * P],
                                                 v_sb[:, j, bass.ds(h, 1), :].rearrange("p a d -> p (a d)"),
                                                 start=(j == 0), stop=(j == i))
                            last.then_inc(S["pv_done"], 1)

                for r in range(4):
                    turn_head(0, r, 0)
                steps(pe, pair)


        def by_head(v, n):
            return v.unsqueeze(2).to_broadcast([P, v.shape[1], n])

        HG = H // G
        GC = HG * HD

        with nc.Block() as block:
            @block.sync
            def _(sp):
                sp.dma_start(w_out_sb[:, :, :], w_out[0].rearrange("(p k) n -> p k n", k=KC)).then_inc(S["w_out_loaded"], 16)

            @block.tensor
            def _(pe):
                pe.wait_ge(S["adt_done"], 1)
                adt_f = adt[:, :, :].rearrange("p t h -> p (t h)")
                pe.matmul(BANK[0][:, 0:NH], tri[:, :], adt_f, start=True, stop=True)
                pe.matmul(BANK[1][:, 0:NH], ones[:, :], adt_f, start=True, stop=True).then_inc(S["cums_done"], 1)
                pe.wait_ge(S["cums_read"], 2)

                def chan(ct, ch):
                    return xbc[:, ct, PAD + ch * P:PAD + (ch + 1) * P]

                def front(ch):
                    if ch:
                        pe.wait_ge(S["ssd_xd"], ch)
                        pe.wait_ge(S["ssd_xsk"], ch)
                    for j in range(NX):
                        last = pe.transpose(BANK[0][:, j * P:(j + 1) * P], chan(j, ch), ident[:, :])
                    last.then_inc(S["ssd_xT"], 1)
                    if ch:
                        pe.wait_ge(S["ssd_b"], ch)
                    for g in range(G):
                        last = pe.transpose(BANK[1][:, g * P:(g + 1) * P], chan(NX + g, ch), ident[:, :])
                    last.then_inc(S["ssd_bT"], 1)
                    if ch:
                        pe.wait_ge(S["ssd_cbm"], ch)
                    for g in range(G):
                        last = pe.matmul(BANK[2][:, g * P:(g + 1) * P], chan(NX + g, ch), chan(NX + G + g, ch),
                                         start=True, stop=True)
                    last.then_inc(S["ssd_cb"], 1)
                    for g in range(G):
                        if ch:
                            pe.wait_ge(S["ssd_arg"], 2 * ch - 1 + g)
                        for j in range(HG):
                            h = g * HG + j
                            last = pe.matmul(BANK[3 + g][:, j * P:(j + 1) * P], adt[:, ch, h:h + 1].to_broadcast([P, P]),
                                             tri[:, :], start=True, stop=True)
                        last.then_inc(S["ssd_rows"], 1)

                def back(ch):
                    if ch:
                        pe.wait_ge(S["ssd_prev"], ch)
                        if ch > 1:
                            pe.wait_ge(S["ssd_y1"], ch)
                        for g in range(G):
                            last = pe.matmul(BANK[6][:, g * GC:(g + 1) * GC], chan(NX + G + g, ch),
                                             state[:, g * GC:(g + 1) * GC], start=True, stop=True)
                        last.then_inc(S["ssd_off"], 1)
                    if ch < NT - 1:
                        pe.wait_ge(S["ssd_b"], ch + 1)
                        pe.wait_ge(S["ssd_xds"], ch + 1)
                        for g in range(G):
                            last = pe.matmul(BANK[7][:, g * GC:(g + 1) * GC], b_tok[ch % 2][:, g * P:(g + 1) * P],
                                             xds[ch % 2][:, g * GC:(g + 1) * GC], start=True, stop=True)
                        last.then_inc(S["ssd_state"], 1)
                    pe.wait_ge(S["ssd_xd"], ch + 1)
                    if ch:
                        pe.wait_ge(S["ssd_y1"], ch)
                    for h in range(H):
                        if h % HG == 0:
                            pe.wait_ge(S["ssd_m"], 2 * ch + h // HG + 1)
                        last = pe.matmul(BANK[5][:, h * HD:(h + 1) * HD],
                                         decay[ch % 2 * 2 + h // HG][:, h % HG * P:(h % HG + 1) * P],
                                         xd[ch % 2][:, h * HD:(h + 1) * HD], start=True, stop=True)
                    last.then_inc(S["ssd_diag"], 1)

                front(0)
                for ch in range(NT):
                    if ch + 1 < NT:
                        front(ch + 1)
                    back(ch)

            @block.scalar
            def _(act):
                act.activation(a_row[:, :], a_row[:, :], ACT.Exp).then_inc(S["a_exp"], 1)
                act.wait_ge(S["dt_pos"], 2)
                act.activation(dt_e[:, :, :], dt_abs[:, :, :], ACT.Exp, scale=-1.0).then_inc(S["dt_exp"], 1)
                act.wait_ge(S["cums_read"], 3)
                act.activation(dec_in[:, :, :], acs[:, :, :], ACT.Exp)
                act.activation(dec_all[:, :, :], tot[:, :, :], ACT.Exp)
                act.activation(dec_out[:, :, :], dec_out[:, :, :], ACT.Exp).then_inc(S["cums_exp"], 1)
                def ssd_square(ch):
                    act.wait_ge(S["ssd_y"], ch + 1)
                    act.wait_ge(S["y_sq_done"], 2 * ch + (2 if ch < NT - 1 else 1))
                    act.activation(junk[:, 0:IN_SSD], zs[:, ch, :], ACT.Square, scale=IN_SSD ** -0.5,
                                   accum_out=stat[:, 3, ch:ch + 1]).then_inc(S["y_sq_done"], 1)

                for ch in range(NT):
                    act.wait_ge(S["ssd_bT"], ch + 1)
                    if ch >= 2:
                        act.wait_ge(S["ssd_state"], ch - 1)
                    act.activation(b_tok[ch % 2][:, :], BANK[1][:, 0:G * P], ACT.Copy).then_inc(S["ssd_b"], 1)
                    for g in range(G):
                        act.wait_ge(S["ssd_arg"], 2 * ch + g + 1)
                        d = decay[ch % 2 * 2 + g][:, :]
                        act.activation(d, d, ACT.Exp).then_inc(S["ssd_exp"], 1)
                    if ch:
                        act.wait_ge(S["y_sq_done"], 2 * ch - 1)
                    act.activation(junk[:, 0:INNER], y_mla[:, ch, :], ACT.Square, scale=INNER ** -0.5,
                                   accum_out=stat[:, 4, ch:ch + 1]).then_inc(S["y_sq_done"], 1)
                    if ch:
                        ssd_square(ch - 1)
                ssd_square(NT - 1)

            @block.vector
            def _(dve):
                def link(ins):
                    step_dve[0] += 1
                    ins.then_inc(S["dve_step"], 1)
                    dve.wait_ge(S["dve_step"], step_dve[0])

                f = lambda t: t[:, :, :]
                link(dve.tensor_tensor(f(dt_x), dt_raw[:, :, :], dtb[:, :].unsqueeze(1).to_broadcast([P, NT, H]), ALU.add))
                dve.tensor_scalar(f(dt_m), f(dt_x), 0.0, None, ALU.max).then_inc(S["dt_pos"], 1)
                dve.scalar_tensor_tensor(f(dt_abs), f(dt_x), -1.0, f(dt_x), ALU.mult, ALU.max).then_inc(S["dt_pos"], 1)
                dve.wait_ge(S["dt_exp"], 1)
                link(dve.tensor_scalar(f(dt_s), f(dt_e), 2.0, None, ALU.add))
                link(dve.reciprocal(f(dt_s), f(dt_s)))
                link(dve.tensor_tensor(f(dt_s), f(dt_s), f(dt_e), ALU.mult))
                link(dve.tensor_tensor(f(dt_z), f(dt_s), f(dt_s), ALU.mult))
                link(dve.tensor_scalar(f(dt_r), f(dt_z), 1.0 / 15, None, ALU.mult))
                for n in (13, 11, 9, 7, 5, 3):
                    link(dve.scalar_tensor_tensor(f(dt_r), f(dt_r), 1.0 / n, f(dt_z), ALU.add, ALU.mult))
                link(dve.scalar_tensor_tensor(f(dt_r), f(dt_r), 1.0, f(dt_s), ALU.add, ALU.mult))
                link(dve.scalar_tensor_tensor(f(dt_all), f(dt_r), 2.0, f(dt_m), ALU.mult, ALU.add))
                dve.wait_ge(S["a_exp"], 1)
                dve.scalar_tensor_tensor(f(adt), f(dt_all), -1.0, a_row[:, :].unsqueeze(1).to_broadcast([P, NT, H]),
                                         ALU.mult, ALU.mult).then_inc(S["adt_done"], 1)
                dve.wait_ge(S["cums_done"], 1)
                flat = lambda t: t[:, :, :].rearrange("p t h -> p (t h)")
                dve.tensor_copy(flat(acs), BANK[0][:, 0:NH]).then_inc(S["cums_read"], 1)
                dve.tensor_copy(flat(tot), BANK[1][:, 0:NH]).then_inc(S["cums_read"], 1)
                dve.wait_ge(S["cums_read"], 2)
                dve.tensor_tensor(flat(dec_out), flat(tot), flat(acs), ALU.subtract).then_inc(S["cums_read"], 1)
                dve.wait_ge(S["cums_exp"], 1)
                heads = lambda v: v.rearrange("p (h d) -> p h d", d=HD)

                def front(ch):
                    dve.wait_ge(S["ssd_xT"], ch + 1)
                    if ch >= 2:
                        dve.wait_ge(S["ssd_diag"], ch - 1)
                        dve.wait_ge(S["ssd_xds"], ch - 1)
                        dve.wait_ge(S["ssd_ysum"], ch - 1)
                    dve.tensor_tensor(heads(xd[ch % 2][:, :]), heads(BANK[0]), by_head(dt_all[:, ch, :], HD), ALU.mult)\
                        .then_inc(S["ssd_xd"], 1)
                    dve.wait_ge(S["ssd_cb"], ch + 1)
                    dve.tensor_tensor(cb[ch % 2][:, :, :], BANK[2][:, 0:G * P].rearrange("p (g l) -> p g l", g=G),
                                      tri[:, :].unsqueeze(1).to_broadcast([P, G, P]), ALU.mult).then_inc(S["ssd_cbm"], 1)
                    for g in range(G):
                        d = decay[ch % 2 * 2 + g][:, :]
                        dve.wait_ge(S["ssd_rows"], 2 * ch + g + 1)
                        link(dve.tensor_tensor(d.rearrange("p (h l) -> p h l", l=P), BANK[3 + g].rearrange("p (h l) -> p h l", l=P),
                                               by_head(acs[:, ch, g * HG:(g + 1) * HG], P), ALU.subtract))
                        dve.tensor_scalar(d, d, 0.0, None, ALU.min).then_inc(S["ssd_arg"], 1)
                    dve.tensor_tensor(heads(xsk[ch % 2][:, :]), heads(BANK[0]), by_head(dsk[:, :], HD), ALU.mult)\
                        .then_inc(S["ssd_xsk"], 1)
                    dve.wait_ge(S["ssd_cbm"], ch + 1)
                    for g in range(G):
                        d = decay[ch % 2 * 2 + g][:, :].rearrange("p (h l) -> p h l", l=P)
                        dve.wait_ge(S["ssd_exp"], 2 * ch + g + 1)
                        dve.tensor_tensor(d, d, cb[ch % 2][:, g:g + 1, :].to_broadcast([P, HG, P]), ALU.mult)\
                            .then_inc(S["ssd_m"], 1)

                def back(ch):
                    if ch < NT - 1:
                        dve.wait_ge(S["ssd_state"], ch + 1)
                        if ch:
                            dve.wait_ge(S["ssd_prevd"], ch)
                            dve.wait_ge(S["ssd_off"], ch)
                            ins = dve.tensor_tensor(state[:, :], BANK[7], state_d[:, :], ALU.add)
                        else:
                            ins = dve.tensor_copy(state[:, :], BANK[7])
                        ins.then_inc(S["ssd_prev"], 1)
                    if ch >= 2:
                        dve.wait_ge(S["ssd_y"], ch - 1)
                    y = y_part[ch % 2][:, :]
                    if ch:
                        dve.wait_ge(S["ssd_off"], ch)
                        link(dve.tensor_tensor(heads(y), heads(BANK[6]), by_head(dec_in[:, ch, :], HD), ALU.mult))
                        dve.wait_ge(S["ssd_diag"], ch + 1)
                        ins = dve.tensor_tensor(y, BANK[5], y, ALU.add)
                    else:
                        dve.wait_ge(S["ssd_diag"], ch + 1)
                        ins = dve.tensor_copy(y, BANK[5])
                    ins.then_inc(S["ssd_y1"], 1)

                front(0)
                for ch in range(NT):
                    if ch + 1 < NT:
                        front(ch + 1)
                    back(ch)

            @block.gpsimd
            def _(pool):
                for name in LATE:
                    pool.sem_clear(S[name])
                pool.wait_ge(S["cums_exp"], 1)
                heads = lambda v: v.rearrange("p (h d) -> p h d", d=HD)

                def decayed(ch):
                    pool.wait_ge(S["ssd_xd"], ch + 1)
                    if ch >= 2:
                        pool.wait_ge(S["ssd_state"], ch - 1)
                    pool.tensor_tensor(heads(xds[ch % 2][:, :]), heads(xd[ch % 2][:, :]), by_head(dec_out[:, ch, :], HD),
                                       ALU.mult).then_inc(S["ssd_xds"], 1)

                decayed(0)
                for ch in range(NT):
                    if ch + 1 < NT:
                        decayed(ch + 1)
                    if 0 < ch < NT - 1:
                        pool.wait_ge(S["ssd_prev"], ch)
                        pool.tensor_tensor(heads(state_d[:, :]), heads(state[:, :]), by_head(dec_all[:, ch, :], HD), ALU.mult)\
                            .then_inc(S["ssd_prevd"], 1)
                    y = y_part[ch % 2][:, :]
                    pool.wait_ge(S["ssd_y1"], ch + 1)
                    pool.wait_ge(S["ssd_xsk"], ch + 1)
                    pool.tensor_tensor(y, y, xsk[ch % 2][:, :], ALU.add).then_inc(S["ssd_ysum"], 1)
                    pool.wait_ge(S["ssd_ysum"], ch + 1)
                    pool.tensor_tensor(zs[:, ch, :], y, zs[:, ch, :], ALU.mult).then_inc(S["ssd_y"], 1)
                for q in (3, 4):
                    inverse_root(pool, q, 0, NT, S["y_sq_done"], 2 * NT)


        wg_v = w_gate[0].rearrange("e (p k) f -> e p k f", k=KC)
        wu_v = w_up[0].rearrange("e (p k) f -> e p k f", k=KC)
        wd_v = w_down[0].rearrange("e (p k) n -> e p k n", k=FC)

        def load_expert(eng, e, r, gu, dn):
            one = lambda v: v[bass.ds(e, 1), :, :, :].rearrange("a p k f -> (a p) k f")
            eng.dma_start(w_gu[r][:, 0, :, :], one(wg_v)).then_inc(gu, 16)
            eng.dma_start(w_gu[r][:, 1, :, :], one(wu_v)).then_inc(gu, 16)
            eng.dma_start(w_dn[r][:, :, :], one(wd_v)).then_inc(dn, 16)

        EB = NG

        with nc.Block() as block:
            @block.sync
            def _(sp):
                def load_x(t):
                    if t >= 2:
                        sp.wait_ge(S["x2_done"], t - 1)
                    sp.dma_start(x_res[t % 2][:, :], x[0, t * P:(t + 1) * P, :]).then_inc(S[f"x_res_loaded{t % 2}"], 16)

                load_x(0)
                load_x(1)
                sp.dma_start(w_r[:, :, 0:NG], w_group_router[0].rearrange("(p k) n -> p k n", k=KC)).then_inc(S["w_r_loaded"], 16)
                sp.dma_start(w_r[:, :, NG:], w_expert_router[0].rearrange("(p k) n -> p k n", k=KC)).then_inc(S["w_r_loaded"], 16)
                load_expert(sp, 0, 0, S["wgu_loaded0"], S["wdn_loaded0"])
                for t in range(NT):
                    sp.wait_ge(S["h2_done"], t + 1)
                    sp.dma_start(h2_rows[t * P:(t + 1) * P, :], h2[t % 2][:, :]).then_inc(S[f"h2_stored{t % 2}"], 16)
                    if t + 2 < NT:
                        load_x(t + 2)
                sp.wait_ge(S["lg_done"], NT)
                load_expert(sp, 1, 1, S["wgu_loaded1"], S["wdn_loaded1"])
                sp.wait_ge(S["h2_stored0"], 16 * NT // 2)
                sp.wait_ge(S["h2_stored1"], 16 * NT // 2)

            @block.gpsimd
            def _(pool):
                for t in range(NT):
                    inverse_root(pool, 5, t, t + 1, S["yo_sq"], t + 1)
                    inverse_root(pool, 6, t, t + 1, S["x2_sq"], t + 1)

            @block.tensor
            def _(pe):
                def cat_T_of(t):
                    pe.wait_ge(S["cat_done"], t + 1)
                    if t:
                        pe.wait_ge(S["catT_act"], t)
                        pe.wait_ge(S["catT_dve"], t)
                    if t >= 4:
                        pe.wait_ge(S["lg_read"], t - 3)
                    for k in range(KC):
                        last = pe.transpose(BANK[k // 4][:, k % 4 * P:(k % 4 + 1) * P], cat[t % 2][:, k::KC], ident[:, :])
                    last.then_inc(S["catT_done"], 1)

                def project(t):
                    pe.wait_ge(S["catT_act"], t + 1)
                    pe.wait_ge(S["catT_dve"], t + 1)
                    if t >= 2:
                        pe.wait_ge(S["y_out"], t - 1)
                    for j in range(D // HALF):
                        for k in range(KC):
                            last = pe.matmul(BANK[2 + t % 2 * 2 + j], cat_T[t % 2][:, k, :],
                                             w_out_sb[:, k, j * HALF:(j + 1) * HALF], start=(k == 0), stop=(k == KC - 1))
                    last.then_inc(S["yo_done"], 1)

                def h2_T_of(t):
                    pe.wait_ge(S["h2_done"], t + 1)
                    if t:
                        pe.wait_ge(S["h2T_act"], t)
                        pe.wait_ge(S["h2T_dve"], t)
                    for k in range(KC):
                        last = pe.transpose(BANK[6 + k // 4][:, k % 4 * P:(k % 4 + 1) * P], h2[t % 2][:, k::KC], ident[:, :])
                    last.then_inc(S["h2T_done"], 1)

                def route(t):
                    pe.wait_ge(S["h2T_act"], t + 1)
                    pe.wait_ge(S["h2T_dve"], t + 1)
                    for k in range(KC):
                        last = pe.matmul(BANK[0][:, 0:NG + E], h2_T[t % 2][:, k, :], w_r[:, k, :], start=(k == 0), stop=(k == KC - 1))
                    last.then_inc(S["lg_done"], 1)

                pe.wait_ge(S["w_out_loaded"], 16)
                pe.wait_ge(S["w_r_loaded"], 32)
                cat_T_of(0)
                for t in range(NT + 2):
                    if t < NT:
                        project(t)
                    if t + 1 < NT:
                        cat_T_of(t + 1)
                    if 1 <= t <= NT:
                        h2_T_of(t - 1)
                    if t >= 2:
                        pe.wait_ge(S["catT_act"], min(t + 2, NT))
                        if t >= 3:
                            pe.wait_ge(S["lg_read"], t - 2)
                        route(t - 2)
                pe.wait_ge(S["rt_both"], 1)
                bf = both.rearrange("p t e -> p (t e)")
                pe.matmul(BANK[1][:, 0:NT * E], tri_lt[:, :], bf, start=True, stop=False)
                pe.matmul(BANK[1][:, 0:NT * E], ones[:, :], before[:, 0:NT, :].rearrange("p t e -> p (t e)"), start=False, stop=True)
                pe.matmul(BANK[2][:, 0:E], ones[:, :], before[:, NT, :], start=True, stop=True).then_inc(S["ranks_done"], 1)
                pe.wait_ge(S["slots_done"], 1)
                for j in range(2 * NT):
                    last = pe.matmul(BANK[3][:, 0:NTILE], row_oh[:, j, :], col_oh[:, j, :], start=(j == 0), stop=(j == 2 * NT - 1))
                last.then_inc(S["idx_done"], 1)

            @block.scalar
            def _(act):
                def cat_half(t):
                    act.wait_ge(S["catT_done"], t + 1)
                    if t >= 2:
                        act.wait_ge(S["yo_done"], t - 1)
                    for k in range(KC // 2):
                        last = act.activation(cat_T[t % 2][:, k, :], BANK[0][:, k * P:(k + 1) * P], ACT.Copy, scale=cat_gain[:, k:k + 1])
                    last.then_inc(S["catT_act"], 1)

                cat_half(0)
                for t in range(NT + 1):
                    if t + 1 < NT:
                        cat_half(t + 1)
                    if t:
                        act.wait_ge(S["h2T_done"], t)
                        if t >= 3:
                            act.wait_ge(S["lg_done"], t - 2)
                        act.activation(h2_T[(t - 1) % 2][:, 0:KC // 2, :], BANK[6].rearrange("p (k n) -> p k n", n=P), ACT.Copy)\
                            .then_inc(S["h2T_act"], 1)
                    if t < NT:
                        act.wait_ge(S["yo_done"], t + 1)
                        if t:
                            act.wait_ge(S["x2_sq"], t)
                        act.activation(junk[:, :], PS[:, 2 + t % 2 * 2:4 + t % 2 * 2, :].rearrange("p a n -> p (a n)"),
                                       ACT.Square, scale=D ** -0.5, accum_out=stat[:, 5, t:t + 1]).then_inc(S["yo_sq"], 1)
                        act.wait_ge(S["x2_done"], t + 1)
                        act.wait_ge(S["yo_sq"], t + 1)
                        act.activation(junk[:, :], x2[:, t, :], ACT.Square, scale=D ** -0.5,
                                       accum_out=stat[:, 6, t:t + 1]).then_inc(S["x2_sq"], 1)
                act.wait_ge(S["route_act"], 1)
                act.activation(g_ex, g_ex, ACT.Exp).then_inc(S["router_exp"], 1)
                act.wait_ge(S["route_act"], 2)
                act.activation(e2, e2, ACT.Exp).then_inc(S["router_exp"], 1)

            @block.vector
            def _(dve):
                def link(ins):
                    step_dve[0] += 1
                    ins.then_inc(S["dve_step"], 1)
                    dve.wait_ge(S["dve_step"], step_dve[0])

                def joined(t):
                    if t >= 2:
                        dve.wait_ge(S["catT_done"], t - 1)
                    dve.tensor_scalar(cat[t % 2][:, 0:IN_SSD], zs[:, t, :], rstd[:, 3, t:t + 1], None, ALU.mult)
                    dve.tensor_scalar(cat[t % 2][:, IN_SSD:], y_mla[:, t, :], rstd[:, 4, t:t + 1], None, ALU.mult)\
                        .then_inc(S["cat_done"], 1)

                def cat_half(t):
                    dve.wait_ge(S["catT_done"], t + 1)
                    if t >= 2:
                        dve.wait_ge(S["yo_done"], t - 1)
                    dve.tensor_tensor(cat_T[t % 2][:, KC // 2:, :], BANK[1].rearrange("p (k n) -> p k n", n=P),
                                      cat_gain[:, KC // 2:].unsqueeze(2).to_broadcast([P, KC // 2, P]), ALU.mult)\
                        .then_inc(S["catT_dve"], 1)

                joined(0)
                joined(1)
                cat_half(0)
                for t in range(NT + 2):
                    if t + 1 < NT:
                        cat_half(t + 1)
                    if 1 <= t <= NT:
                        dve.wait_ge(S["h2T_done"], t)
                        if t >= 3:
                            dve.wait_ge(S["lg_done"], t - 2)
                        dve.tensor_copy(h2_T[(t - 1) % 2][:, KC // 2:, :], BANK[7].rearrange("p (k n) -> p k n", n=P))\
                            .then_inc(S["h2T_dve"], 1)
                    if t >= 2:
                        dve.wait_ge(S["lg_done"], t - 1)
                        dve.tensor_tensor(logits[:, t - 2, :], BANK[0][:, 0:NG + E], rb_row[:, :], ALU.add).then_inc(S["lg_read"], 1)
                    if t < NT:
                        dve.wait_ge(S["rstd_done"], NT + 4 + 2 * t + 1)
                        if t >= 2:
                            dve.wait_ge(S[f"h2_stored{t % 2}"], 16 * (t // 2))
                            dve.wait_ge(S["h2T_done"], t - 1)
                        yb = PS[:, 2 + t % 2 * 2:4 + t % 2 * 2, :].rearrange("p a n -> p (a n)")
                        dve.scalar_tensor_tensor(y_sc[t % 2][:, :], yb, rstd[:, 5, t:t + 1], G1[:, :], ALU.mult, ALU.mult)\
                            .then_inc(S["y_out"], 1)
                        dve.wait_ge(S["y_out"], t + 1)
                        dve.wait_ge(S[f"x_res_loaded{t % 2}"], 16 * (t // 2 + 1))
                        dve.tensor_tensor(x2[:, t, :], y_sc[t % 2][:, :], x_res[t % 2][:, :], ALU.add).then_inc(S["x2_done"], 1)
                        dve.wait_ge(S["rstd_done"], NT + 4 + 2 * t + 2)
                        dve.scalar_tensor_tensor(h2[t % 2][:, :], x2[:, t, :], rstd[:, 6, t:t + 1], A2[:, :], ALU.mult, ALU.mult)\
                            .then_inc(S["h2_half"], 1)
                        dve.wait_ge(S["h2_half"], t + 1)
                        dve.tensor_tensor(h2[t % 2][:, :], h2[t % 2][:, :], B2[:, :], ALU.add).then_inc(S["h2_done"], 1)
                    if t + 2 < NT:
                        joined(t + 2)

                dve.wait_ge(S["lg_read"], NT)
                for u in range(2):
                    dve.wait_ge(S[f"h2_stored{u}"], 16 * NT // 2)
                Lg, Le = logits[:, :, 0:NG], logits[:, :, EB:]
                wide = lambda v, n: v.unsqueeze(2).to_broadcast([P, NT, n])
                iota = lambda n: iota_row[:, 0:n].unsqueeze(1).to_broadcast([P, NT, n])

                def first_of_max(v, top, tmp, onehot, n):
                    link(dve.tensor_reduce(top, v, AX_X, ALU.max))
                    link(dve.tensor_tensor(tmp, v, wide(top, n), ALU.is_equal))
                    link(dve.scalar_tensor_tensor(tmp, tmp, -64.0, iota(n), ALU.mult, ALU.add))
                    link(dve.tensor_reduce(mn, tmp, AX_X, ALU.min))
                    link(dve.tensor_tensor(onehot, tmp, wide(mn, n), ALU.is_equal))

                first_of_max(Lg, g_max, g_cand, g_oh, NG)
                dve.tensor_tensor(g_ex, Lg, wide(g_max, NG), ALU.subtract).then_inc(S["route_act"], 1)
                link(dve.tensor_scalar(g_eq, g_oh, 1.0, -NEG, ALU.subtract, ALU.mult))
                grouped = lambda v: v.rearrange("p t (g e) -> p t g e", e=EPG)
                link(dve.tensor_tensor(grouped(lm), grouped(Le), g_eq.unsqueeze(3).to_broadcast([P, NT, NG, EPG]), ALU.add))
                first_of_max(lm, m1, cand, oh1, E)
                link(dve.scalar_tensor_tensor(lm2, oh1, -3.0e38, lm, ALU.mult, ALU.add))
                first_of_max(lm2, m2, cand, oh2, E)
                dve.tensor_tensor(e2, m2, m1, ALU.subtract).then_inc(S["route_act"], 1)
                link(dve.tensor_tensor(both, oh1, oh2, ALU.add))
                dve.memset(before[:, 0, :], 0.0)
                dve.memset(zero32, 0.0)
                link(dve.tensor_copy(before[:, 1, :], both[:, 0, :]))
                for t in range(1, NT):
                    ins = dve.tensor_tensor(before[:, t + 1, :], before[:, t, :], both[:, t, :], ALU.add)
                    if t < NT - 1:
                        link(ins)
                ins.then_inc(S["rt_both"], 1)
                dve.wait_ge(S["router_exp"], 1)
                link(dve.tensor_reduce(g_sum, g_ex, AX_X, ALU.add))
                dve.wait_ge(S["router_exp"], 2)
                link(dve.scalar_tensor_tensor(den, e2, 1.0, g_sum, ALU.add, ALU.mult))
                link(dve.reciprocal(wts[:, 0, :], den))
                dve.tensor_tensor(wts[:, 1, :], wts[:, 0, :], e2, ALU.mult)
                for j in range(2):
                    dve.tensor_scalar(place_id[:, j, :], tok_id[:, :], 2.0, float(1 + j), ALU.mult, ALU.add)
                link(dve.tensor_scalar(thr, iota_row[:, 1:NT + 1], float(P), None, ALU.mult))
                dve.tensor_scalar(lo128, iota_row[:, 0:E], float(P), None, ALU.mult)
                dve.wait_ge(S["ranks_done"], 1)
                link(dve.tensor_copy(cnt, BANK[2][:, 0:E]))
                link(dve.tensor_tensor(cmp_n, cnt.unsqueeze(2).to_broadcast([P, E, NT]),
                                       thr.unsqueeze(1).to_broadcast([P, E, NT]), ALU.is_gt))
                link(dve.tensor_reduce(n_over, cmp_n, AX_X, ALU.add))
                link(dve.tensor_tensor_scan(incl, n_over, zero32, 0.0, ALU.add, ALU.add))
                link(dve.tensor_tensor(base_t, incl, n_over, ALU.subtract))
                link(dve.tensor_scalar(base_t, base_t, float(E - 1), float(P), ALU.add, ALU.mult))
                link(dve.tensor_tensor(dlt, base_t, lo128, ALU.subtract))
                ex = lambda v: v.unsqueeze(1).to_broadcast([P, NT, E])
                rk = BANK[1][:, 0:NT * E].rearrange("p (t e) -> p t e", e=E)
                link(dve.tensor_scalar(over, rk, float(P), None, ALU.is_ge))
                link(dve.tensor_tensor(over, over, ex(dlt), ALU.mult))
                link(dve.tensor_tensor(rank, rk, over, ALU.add))
                link(dve.tensor_tensor(rank, rank, ex(lo128), ALU.add))
                for j, oh in enumerate((oh1, oh2)):
                    link(dve.tensor_tensor(cand, oh, rank, ALU.mult))
                    link(dve.tensor_reduce(slot_f[:, j, :], cand, AX_X, ALU.add))
                link(dve.tensor_copy(slot_i[:, :, :], slot_f))
                link(dve.tensor_scalar(col_i, slot_i[:, :, :], 7, None, ALU.logical_shift_right))
                link(dve.tensor_scalar(row_i, slot_i[:, :, :], P - 1, None, ALU.bitwise_and))
                link(dve.tensor_copy(col_f, col_i))
                link(dve.tensor_copy(row_f, row_i))
                rf, cf = (v.rearrange("p j t -> p (j t)") for v in (row_f, col_f))
                link(dve.tensor_tensor(row_oh, iota_row[:, :].unsqueeze(1).to_broadcast([P, 2 * NT, P]),
                                       rf.unsqueeze(2).to_broadcast([P, 2 * NT, P]), ALU.is_equal))
                link(dve.tensor_tensor(col_oh, iota_row[:, 0:NTILE].unsqueeze(1).to_broadcast([P, 2 * NT, NTILE]),
                                       cf.unsqueeze(2).to_broadcast([P, 2 * NT, NTILE]), ALU.is_equal))
                for j in range(2):
                    v = col_oh[:, j * NT:(j + 1) * NT, :]
                    ins = dve.tensor_tensor(v, v, place_id[:, j, :].unsqueeze(2).to_broadcast([P, NT, NTILE]), ALU.mult)
                ins.then_inc(S["slots_done"], 1)
                link(dve.tensor_tensor(cmp, iota_row[:, 0:XT].unsqueeze(2).to_broadcast([P, XT, E]),
                                       incl.unsqueeze(1).to_broadcast([P, XT, E]), ALU.is_ge))
                link(dve.tensor_reduce(meta_f[:, 0:XT], cmp, AX_X, ALU.add))
                link(dve.tensor_scalar(meta_f[:, 0:XT], meta_f[:, 0:XT], float(E - 1), None, ALU.min))
                link(dve.tensor_copy(meta_f[:, XT:], incl[:, E - 1:E]))
                dve.tensor_copy(meta_i[:, :], meta_f)
                dve.wait_ge(S["idx_done"], 1)
                link(dve.tensor_scalar(put_f[:, 0, :], BANK[3][:, 0:NTILE], 0.0, float(2 * T + 1), ALU.is_equal, ALU.mult))
                link(dve.scalar_tensor_tensor(put_f[:, 1, :], BANK[3][:, 0:NTILE], -1.0, put_f[:, 0, :], ALU.add, ALU.add))
                link(dve.tensor_copy(dst_i[:, :], put_f[:, 1, :]))
                dve.tensor_scalar(idx_i[:, :], dst_i[:, :], 1, None, ALU.logical_shift_right).then_inc(S["idx_read"], 1)
                dve.wait_ge(S["idx_read"], 1)


        RING = 4
        assert E % RING == 0 and E > RING
        MORE = 2
        TILES = E + MORE
        LATER_CREDIT = {"v_down": 2}

        with nc.Block() as block:
            def rounds(eng, four):
                four(0, range(RING), True, False)
                with eng.Fori(1, E // RING - 1) as i:
                    four(i * RING, range(RING), False, False)
                four(E - RING, range(RING + MORE), False, True)

            def extra(eng, one):
                n_extra = eng.snap(eng.value_load(meta_i[0:1, XT:XT + 1], min_val=0, max_val=XT))
                with eng.Fori(MORE // 2, XT // 2) as i:
                    for u in range(2):
                        with eng.If(i * 2 + u < n_extra):
                            one(i, u)

            @block.sync
            def _(sp):
                def four(n0, us, first, last):
                    for u in us:
                        if first and u < 2:
                            continue
                        if not first:
                            sp.wait_ge(S["dn_done"], n0 + u - RING + 1)
                        e, r = n0 + u, u % RING
                        if u >= RING:
                            e = sp.value_load(meta_i[0:1, u - RING:u - RING + 1], min_val=0, max_val=E - 1)
                        load_expert(sp, e, r, S[f"wgu_loaded{r}"], S[f"wdn_loaded{r}"])

                rounds(sp, four)
                sp.wait_ge(S["dn_done"], TILES)

                def one(i, u):
                    j = i * 2 + u
                    e = sp.value_load(meta_i[0:1, bass.ds(j, 1)], min_val=0, max_val=E - 1)
                    sp.wait_ge(S["v_down"], j + 1 - MORE)
                    load_expert(sp, e, u, S[f"v_gu{u}"], S[f"v_dn{u}"])

                extra(sp, one)

            @block.gpsimd
            def _(pool):
                pool.sem_inc(S["v_down"], LATER_CREDIT["v_down"])

                def gather(tile, u, step, value, loaded):
                    pool.tensor_copy(idx_now[u][:, :], idx_i[:, bass.ds(tile, 1)]).then_inc(step, 1)
                    pool.wait_ge(step, value)
                    pool.sem_inc(S["gathers_begun"], 1)
                    pool.indirect_dma_start(x_g[u][:, :], None, h2_rows,
                                            bass.IndirectOffsetOnAxis(ap=idx_now[u][:, :], axis=0),
                                            bounds_check=T - 1, oob_is_err=False).then_inc(loaded, 16)

                def scatter(tile, b, value, stored):
                    pool.tensor_copy(dst_now[b][:, :], dst_i[:, bass.ds(tile, 1)]).then_inc(S["dst_step"], 1)
                    pool.wait_ge(S["dst_step"], value)
                    pool.sem_inc(S["gathers_begun"], 1)
                    pool.indirect_dma_start(y_rows, bass.IndirectOffsetOnAxis(ap=dst_now[b][:, :], axis=0),
                                            y_e[b][:, :], None,
                                            bounds_check=2 * T - 1, oob_is_err=False).then_inc(stored, 16)

                def scatter_of(n0, u, first):
                    n, b = n0 + u, u % 2
                    pool.wait_ge(S["ye_act"], n + 1)
                    pool.wait_ge(S["ye_dve"], n + 1)
                    if not (first and u < 2):
                        pool.wait_ge(S[f"ye_stored{b}"], (n - b) * 8)
                    scatter(n, b, n + 1, S[f"ye_stored{b}"])

                def four(n0, us, first, last):
                    for u in us:
                        if not (first and u < 2):
                            pool.wait_ge(S["tx_done"], n0 + u - 1)
                            pool.wait_ge(S["idx_read"], 1)
                        gather(n0 + u, u % 2, S["idx_step"], n0 + u + 1, S[f"xg_loaded{u % 2}"])
                        if not (first and u < 3):
                            scatter_of(n0, u - 3, first)

                rounds(pool, four)
                for u in range(RING + MORE - 3, RING + MORE):
                    scatter_of(E - RING, u, False)
                pool.wait_ge(S["tx_done"], TILES)

                def one(i, u):
                    j = i * 2 + u
                    pool.wait_ge(S["v_down"], j + 1 - MORE)
                    pool.wait_ge(S["idx_read"], 1)
                    gather(E + j, u, S["v_idx"], j + 1 - MORE, S[f"v_xg{u}"])
                    pool.wait_ge(S["v_ya"], j + 1 - MORE)
                    pool.wait_ge(S["v_yd"], j + 1 - MORE)
                    scatter(E + j, u, j + E + 1, S["v_stored"])
                    pool.wait_ge(S["v_stored"], (j - MORE) * 16 + 16)
                    pool.sem_inc(S["gathers_begun"], 1)

                for b in range(2):
                    pool.wait_ge(S[f"ye_stored{b}"], 16 * TILES // 2)
                extra(pool, one)

            @block.tensor
            def _(pe):
                def tokens_T(u):
                    for k in range(KC):
                        last = pe.transpose(BANK[k // 4][:, k % 4 * P:(k % 4 + 1) * P], x_g[u][:, k::KC], ident[:, :])
                    return last

                def gate_up(b, r, bank):
                    for k in range(KC):
                        last = pe.matmul(BANK[bank], xg_T[b][:, k, :], w_gu[r][:, :, k, :], start=(k == 0), stop=(k == KC - 1))
                    return last

                def hidden_T(b):
                    for k in range(FC):
                        last = pe.transpose(BANK[4][:, k * P:(k + 1) * P], hid[b][:, k::FC], ident[:, :])
                    return last

                def down(b, r):
                    for j in range(D // HALF):
                        for k in range(FC):
                            last = pe.matmul(BANK[5 + j], hid_T[b][:, k, :], w_dn[r][:, k, j * HALF:(j + 1) * HALF],
                                             start=(k == 0), stop=(k == FC - 1))
                    return last

                def tokens(n0, u):
                    n = n0 + u
                    pe.wait_ge(S[f"xg_loaded{u % 2}"], (n - u % 2) * 8 + 16)
                    tokens_T(u % 2).then_inc(S["tx_done"], 1)

                pe.wait_ge(S["xg_loaded0"], 16)
                tokens_T(0).then_inc(S["tx_done"], 1)

                def four(n0, us, first, last):
                    for u in us:
                        n, b, r = n0 + u, u % 2, u % RING
                        pe.wait_ge(S["tx_act"], n + 1)
                        pe.wait_ge(S["tx_dve"], n + 1)
                        if not (first and u < 2):
                            pe.wait_ge(S["hid_done"], n - 1)
                        pe.wait_ge(S[f"wgu_loaded{r}"], n0 * 8 + u // RING * 32 + 32)
                        gate_up(b, r, 2 + b).then_inc(S["gu_done"], 1)
                        if not (last and u == us[-1]):
                            tokens(n0, u + 1)
                        if not (first and u == 0):
                            down_of(n - 1, (u - 1) % 2, (u - 1) % RING, first and u == 1)
                        pe.wait_ge(S["hid_done"], n + 1)
                        if not (first and u == 0):
                            pe.wait_ge(S["th_read"], n)
                        hidden_T(b).then_inc(S["th_done"], 1)

                def down_of(n, b, r, first):
                    pe.wait_ge(S["th_read"], n + 1)
                    if not first:
                        pe.wait_ge(S["ye_act"], n)
                        pe.wait_ge(S["ye_dve"], n)
                    pe.wait_ge(S[f"wdn_loaded{r}"], (n - r) * 4 + 16)
                    down(b, r).then_inc(S["dn_done"], 1)

                rounds(pe, four)
                down_of(TILES - 1, 1, (TILES - 1) % RING, False)

                def one(i, u):
                    j = i * 2 + u
                    pe.wait_ge(S[f"v_xg{u}"], (i - MORE // 2) * 16 + 16)
                    tokens_T(u).then_inc(S["v_tx"], 1)
                    pe.wait_ge(S["v_txa"], j + 1 - MORE)
                    pe.wait_ge(S["v_txd"], j + 1 - MORE)
                    pe.wait_ge(S[f"v_gu{u}"], (i - MORE // 2) * 32 + 32)
                    gate_up(u, u, 2 + u).then_inc(S["v_gud"], 1)
                    pe.wait_ge(S["v_hid"], j + 1 - MORE)
                    hidden_T(u).then_inc(S["v_th"], 1)
                    pe.wait_ge(S["v_thr"], j + 1 - MORE)
                    pe.wait_ge(S[f"v_dn{u}"], (i - MORE // 2) * 16 + 16)
                    down(u, u).then_inc(S["v_down"], 1)

                pe.wait_ge(S["ye_act"], TILES)
                pe.wait_ge(S["ye_dve"], TILES)
                extra(pe, one)

            @block.scalar
            def _(act):
                def tx(b):
                    return act.activation(xg_T[b][:, 0:KC // 2, :], BANK[0].rearrange("p (k n) -> p k n", n=P), ACT.Copy)

                def silu(b):
                    return act.activation(hid_s[b][:, :], BANK[2 + b][:, 0:FF], ACT.Silu)

                def out(b):
                    return act.activation(y_e[b][:, 0:HALF], BANK[5], ACT.Copy)

                def y_of(n0, u, first):
                    n, b = n0 + u, u % 2
                    act.wait_ge(S["dn_done"], n + 1)
                    if not (first and u < 2):
                        act.wait_ge(S[f"ye_stored{b}"], (n - b) * 8)
                    out(b).then_inc(S["ye_act"], 1)

                act.wait_ge(S["tx_done"], 1)
                tx(0).then_inc(S["tx_act"], 1)

                def four(n0, us, first, last):
                    for u in us:
                        n, b = n0 + u, u % 2
                        act.wait_ge(S["gu_done"], n + 1)
                        if not (first and u < 2):
                            act.wait_ge(S["hid_done"], n - 1)
                        silu(b).then_inc(S["silu_done"], 1)
                        if not (last and u == us[-1]):
                            act.wait_ge(S["tx_done"], n + 2)
                            if not (first and u == 0):
                                act.wait_ge(S["gu_done"], n)
                            tx(1 - b).then_inc(S["tx_act"], 1)
                        if not (first and u == 0):
                            y_of(n0, u - 1, first)

                rounds(act, four)
                y_of(E - RING, RING + MORE - 1, False)

                def one(i, u):
                    j = i * 2 + u
                    act.wait_ge(S["v_tx"], j + 1 - MORE)
                    tx(u).then_inc(S["v_txa"], 1)
                    act.wait_ge(S["v_gud"], j + 1 - MORE)
                    silu(u).then_inc(S["v_silu"], 1)
                    act.wait_ge(S["v_down"], j + 1 - MORE + LATER_CREDIT["v_down"])
                    out(u).then_inc(S["v_ya"], 1)

                for b in range(2):
                    act.wait_ge(S[f"ye_stored{b}"], 16 * TILES // 2)
                extra(act, one)

            @block.vector
            def _(dve):
                def tx(b):
                    return dve.tensor_copy(xg_T[b][:, KC // 2:, :], BANK[1].rearrange("p (k n) -> p k n", n=P))

                def gated(b):
                    return dve.tensor_tensor(hid[b][:, :], BANK[2 + b][:, FF:], hid_s[b][:, :], ALU.mult)

                def th(b):
                    return dve.tensor_copy(hid_T[b][:, :, :], BANK[4][:, 0:FF].rearrange("p (k n) -> p k n", n=P))

                def out(b):
                    return dve.tensor_copy(y_e[b][:, HALF:], BANK[6])

                def y_of(n0, u, first):
                    n, b = n0 + u, u % 2
                    dve.wait_ge(S["dn_done"], n + 1)
                    if not (first and u < 2):
                        dve.wait_ge(S[f"ye_stored{b}"], (n - b) * 8)
                    out(b).then_inc(S["ye_dve"], 1)

                dve.wait_ge(S["tx_done"], 1)
                tx(0).then_inc(S["tx_dve"], 1)

                def four(n0, us, first, last):
                    for u in us:
                        n, b = n0 + u, u % 2
                        dve.wait_ge(S["silu_done"], n + 1)
                        if not (first and u < 2):
                            dve.wait_ge(S["th_done"], n - 1)
                        gated(b).then_inc(S["hid_done"], 1)
                        if not (last and u == us[-1]):
                            dve.wait_ge(S["tx_done"], n + 2)
                            tx(1 - b).then_inc(S["tx_dve"], 1)
                        if not (first and u == 0):
                            y_of(n0, u - 1, first)
                        dve.wait_ge(S["th_done"], n + 1)
                        if not (first and u < 2):
                            dve.wait_ge(S["dn_done"], n - 1)
                        th(b).then_inc(S["th_read"], 1)

                rounds(dve, four)
                y_of(E - RING, RING + MORE - 1, False)
                for b in range(2):
                    dve.wait_ge(S[f"ye_stored{b}"], 16 * TILES // 2)

                def one(i, u):
                    j = i * 2 + u
                    dve.wait_ge(S["v_tx"], j + 1 - MORE)
                    tx(u).then_inc(S["v_txd"], 1)
                    dve.wait_ge(S["v_silu"], j + 1 - MORE)
                    gated(u).then_inc(S["v_hid"], 1)
                    dve.wait_ge(S["v_th"], j + 1 - MORE)
                    th(u).then_inc(S["v_thr"], 1)
                    dve.wait_ge(S["v_down"], j + 1 - MORE + LATER_CREDIT["v_down"])
                    out(u).then_inc(S["v_yd"], 1)

                extra(dve, one)

        with nc.Block() as block:
            @block.gpsimd
            def _(pool):
                for t in range(NT):
                    inverse_root(pool, 7, t, t + 1, S["ysum_sq"], t + 1)

            @block.scalar
            def _(act):
                def scaled(t):
                    act.wait_ge(S[f"yg_loaded{t % NY}"], 16 * (t // NY + 1))
                    if t >= NY:
                        act.wait_ge(S[f"o_stored{t % NY}"], 16 * (t // NY))
                    act.activation(y_sum[t % NY][:, :], y_g[t % NY][:, 0, :], ACT.Copy, scale=wts[:, 0, t:t + 1])\
                        .then_inc(S["ya_scaled"], 1)

                scaled(0)
                for t in range(NT):
                    if t + 1 < NT:
                        scaled(t + 1)
                    act.wait_ge(S["ysum_done"], t + 1)
                    if t:
                        act.wait_ge(S["ysum_sq"], t)
                    act.activation(junk[:, :], y_sum[t % NY][:, :], ACT.Square, scale=D ** -0.5,
                                   accum_out=stat[:, 7, t:t + 1]).then_inc(S["ysum_sq"], 1)

            @block.vector
            def _(dve):
                def summed(t):
                    dve.wait_ge(S["ya_scaled"], t + 1)
                    dve.scalar_tensor_tensor(y_sum[t % NY][:, :], y_g[t % NY][:, 1, :], wts[:, 1, t:t + 1],
                                             y_sum[t % NY][:, :], ALU.mult, ALU.add).then_inc(S["ysum_done"], 1)

                summed(0)
                for t in range(NT):
                    if t + 1 < NT:
                        summed(t + 1)
                    y = y_sum[t % NY][:, :]
                    dve.wait_ge(S["rstd_done"], 3 * NT + 4 + t + 1)
                    dve.scalar_tensor_tensor(y, y, rstd[:, 7, t:t + 1], G2[:, :], ALU.mult, ALU.mult).then_inc(S["o_scaled"], 1)
                    dve.wait_ge(S["o_scaled"], t + 1)
                    dve.tensor_tensor(y, y, x2[:, t, :], ALU.add).then_inc(S["o_done"], 1)

            @block.sync
            def _(sp):
                def load(t):
                    if t >= NY:
                        sp.wait_ge(S["ysum_done"], t - NY + 1)
                    sp.dma_start(y_g[t % NY][:, :, :], y_rows[2 * t * P:2 * (t + 1) * P, :].rearrange("(p j) d -> p j d", j=2))\
                        .then_inc(S[f"yg_loaded{t % NY}"], 16)

                for t in range(NY):
                    load(t)
                for t in range(NT):
                    sp.wait_ge(S["o_done"], t + 1)
                    sp.dma_start(out[0, t * P:(t + 1) * P, :], y_sum[t % NY][:, :]).then_inc(S[f"o_stored{t % NY}"], 16)
                    if t + NY < NT:
                        load(t + NY)
                for u in range(NY):
                    sp.wait_ge(S[f"o_stored{u}"], 16 * NT // NY)


_INS = ["x", "c", "positions", "ada_w", "ada_b", "pre_norm_mix", "post_norm_mix", "pre_norm_ffn",
        "post_norm_ffn", "w_in", "conv_w", "conv_b", "dt_bias", "a_log", "d_skip", "ssd_norm", "q_norm",
        "w_uq", "kv_norm", "w_ukv", "mla_out_norm", "w_out", "w_group_router", "b_group_router",
        "w_expert_router", "b_expert_router", "w_gate", "w_up", "w_down"]


def kernel(**inputs):
    import numpy as _np
    import concourse.bacc as _bacc
    from concourse import mybir as _mybir
    from concourse.bass_utils import run_bass_kernel_spmd as _run

    nc = _bacc.Bacc("TRN2", target_bir_lowering=False, num_devices=1)
    arrays, args = {}, []
    for name in _INS:
        a = _np.ascontiguousarray(inputs[name])
        arrays[f"in_{name}_dram"] = a
        args.append(nc.dram_tensor(f"in_{name}_dram", a.shape, _mybir.dt.from_np(a.dtype), kind="ExternalInput").ap())
    shape = inputs["x"].shape
    args.append(nc.dram_tensor("out_0_dram", shape, _mybir.dt.float32, kind="ExternalOutput").ap())
    hybrid_block(nc, *args)
    r = _run(nc, [arrays], core_ids=[0])
    return r.results[0]["out_0_dram"]
```
